# Optimizing a Trainium2 kernel written in Bass

```python
import jax, jax.numpy as jnp
from jax import lax
import numpy as np

D_MODEL = 2048
BATCH = 1
SEQ = 256
DEPTH = 1

HEAD_DIM = 128
N_HEADS_FOX = 8
N_HEADS_MOBA = 8
WIDTH_FOX = N_HEADS_FOX * HEAD_DIM
WIDTH_MOBA = N_HEADS_MOBA * HEAD_DIM
FOX_Q_BLOCK = 128
MOBA_BLOCK = 256
MOBA_TOPK = 3
MOBA_Q_CHUNK = 16
D_FF = -(-(8 * D_MODEL) // (3 * 256)) * 256
ROPE_THETA = 10000.0
RMS_EPS = 1e-6
IN_COLS = 3 * WIDTH_FOX + 3 * WIDTH_MOBA + N_HEADS_FOX + 2 * D_MODEL

kernel_name = "hybrid_fox_moba_gated_swiglu"

def rms_norm(x, g):
    xf = x.astype(jnp.float32)
    y = xf * lax.rsqrt(jnp.mean(xf * xf, axis=-1, keepdims=True) + RMS_EPS)
    return (y * g.astype(jnp.float32)).astype(x.dtype)

def to_heads(t, n_heads):
    b, s, _ = t.shape
    return t.reshape(b, s, n_heads, HEAD_DIM).transpose(0, 2, 1, 3)

def from_heads(t):
    b, h, s, d = t.shape
    return t.transpose(0, 2, 1, 3).reshape(b, s, h * d)

def rotary(t):
    s = t.shape[2]
    half = HEAD_DIM // 2
    inv_freq = ROPE_THETA ** (-jnp.arange(half, dtype=jnp.float32) / half)
    ang = jnp.arange(s, dtype=jnp.float32)[:, None] * inv_freq[None, :]
    cos, sin = jnp.cos(ang), jnp.sin(ang)
    tf = t.astype(jnp.float32)
    t1, t2 = tf[..., :half], tf[..., half:]
    out = jnp.concatenate([t1 * cos - t2 * sin, t2 * cos + t1 * sin], axis=-1)
    return out.astype(t.dtype)

def forgetting_attention(q, k, v, log_f):
    b, h, s, _ = q.shape
    c = jnp.cumsum(log_f, axis=-1)
    scale = HEAD_DIM ** -0.5
    kpos = jnp.arange(s)

    def block(start):
        qb = lax.dynamic_slice_in_dim(q, start, FOX_Q_BLOCK, axis=2)
        cb = lax.dynamic_slice_in_dim(c, start, FOX_Q_BLOCK, axis=2)
        qpos = start + jnp.arange(FOX_Q_BLOCK)
        logits = jnp.einsum('bhqd,bhkd->bhqk', qb, k,
                            preferred_element_type=jnp.float32) * scale
        logits = logits + (cb[..., :, None] - c[..., None, :])
        logits = jnp.where(kpos[None, :] <= qpos[:, None], logits, -jnp.inf)
        p = jax.nn.softmax(logits, axis=-1)
        return jnp.einsum('bhqk,bhkd->bhqd', p.astype(v.dtype), v)

    starts = jnp.arange(0, s, FOX_Q_BLOCK)
    out = lax.map(block, starts)
    return out.transpose(1, 2, 0, 3, 4).reshape(b, h, s, HEAD_DIM)

def moba_attention(q, k, v):
    b, h, s, _ = q.shape
    n_blocks = -(-s // MOBA_BLOCK)
    s_pad = n_blocks * MOBA_BLOCK
    pad = ((0, 0), (0, 0), (0, s_pad - s), (0, 0))
    kp = jnp.pad(k, pad)
    vp = jnp.pad(v, pad)
    kb = kp.reshape(b, h, n_blocks, MOBA_BLOCK, HEAD_DIM)
    vb = vp.reshape(b, h, n_blocks, MOBA_BLOCK, HEAD_DIM)
    k_mean = jnp.mean(kb.astype(jnp.float32), axis=3)
    topk = min(MOBA_TOPK, n_blocks)
    scale = HEAD_DIM ** -0.5
    block_ids = jnp.arange(n_blocks)
    gather = jax.vmap(jax.vmap(lambda tbl, ids: tbl[ids]))

    def chunk(start):
        qc = lax.dynamic_slice_in_dim(q, start, MOBA_Q_CHUNK, axis=2)
        blk = start // MOBA_BLOCK
        qpos = start + jnp.arange(MOBA_Q_CHUNK)
        gate = jnp.einsum('bhqd,bhnd->bhqn', qc.astype(jnp.float32), k_mean)
        gate = jnp.where(block_ids < blk, gate, -jnp.inf)
        _, idx = lax.top_k(gate, topk)
        valid = idx < blk
        k_sel = gather(kb, idx)
        v_sel = gather(vb, idx)
        s_sel = jnp.einsum('bhqd,bhqnkd->bhqnk', qc, k_sel,
                           preferred_element_type=jnp.float32) * scale
        s_sel = jnp.where(valid[..., None], s_sel, -jnp.inf)
        s_sel = s_sel.reshape(b, h, MOBA_Q_CHUNK, topk * MOBA_BLOCK)
        k_own = lax.dynamic_slice_in_dim(kp, blk * MOBA_BLOCK, MOBA_BLOCK, axis=2)
        v_own = lax.dynamic_slice_in_dim(vp, blk * MOBA_BLOCK, MOBA_BLOCK, axis=2)
        kpos = blk * MOBA_BLOCK + jnp.arange(MOBA_BLOCK)
        s_own = jnp.einsum('bhqd,bhkd->bhqk', qc, k_own,
                           preferred_element_type=jnp.float32) * scale
        s_own = jnp.where(kpos[None, :] <= qpos[:, None], s_own, -jnp.inf)
        p = jax.nn.softmax(jnp.concatenate([s_sel, s_own], axis=-1), axis=-1)
        p_sel = p[..., :topk * MOBA_BLOCK].reshape(b, h, MOBA_Q_CHUNK, topk, MOBA_BLOCK)
        p_own = p[..., topk * MOBA_BLOCK:]
        out = (jnp.einsum('bhqnk,bhqnkd->bhqd', p_sel.astype(v.dtype), v_sel)
               + jnp.einsum('bhqk,bhkd->bhqd', p_own.astype(v.dtype), v_own))
        return out

    starts = jnp.arange(0, s, MOBA_Q_CHUNK)
    out = lax.map(chunk, starts)
    return out.transpose(1, 2, 0, 3, 4).reshape(b, h, s, HEAD_DIM)

def split_offsets():
    sizes = [WIDTH_FOX] * 3 + [WIDTH_MOBA] * 3 + [N_HEADS_FOX, D_MODEL]
    offs, acc = [], 0
    for sz in sizes:
        acc += sz
        offs.append(acc)
    return offs

def setup_inputs(seed: int = 0) -> dict:
    key = jax.random.key(seed)
    ks = jax.random.split(key, 12)
    f32 = jnp.float32

    def nrm(k, shape, fan_in):
        return jax.random.normal(k, shape, f32) * (fan_in ** -0.5)

    x = jax.random.normal(ks[0], (BATCH, SEQ, D_MODEL), f32)
    norm_mix = 1.0 + 0.02 * jax.random.normal(ks[1], (DEPTH, D_MODEL), f32)
    w_in = nrm(ks[2], (DEPTH, D_MODEL, IN_COLS), D_MODEL)
    b_forget = (jnp.linspace(1.0, 5.0, N_HEADS_FOX, dtype=f32)[None, :]
                + 0.1 * jax.random.normal(ks[3], (DEPTH, N_HEADS_FOX), f32))
    w_o_fox = nrm(ks[4], (DEPTH, WIDTH_FOX, D_MODEL), WIDTH_FOX)
    w_o_moba = nrm(ks[5], (DEPTH, WIDTH_MOBA, D_MODEL), WIDTH_MOBA)
    w_out = nrm(ks[6], (DEPTH, D_MODEL, D_MODEL), D_MODEL)
    norm_ffn = 1.0 + 0.02 * jax.random.normal(ks[7], (DEPTH, D_MODEL), f32)
    w_gate_up = nrm(ks[8], (DEPTH, D_MODEL, 2 * D_FF), D_MODEL)
    w_down = nrm(ks[9], (DEPTH, D_FF, D_MODEL), D_FF)
    norm_final = 1.0 + 0.02 * jax.random.normal(ks[10], (D_MODEL,), f32)
    return {"x": x, "norm_mix": norm_mix, "w_in": w_in, "b_forget": b_forget,
            "w_o_fox": w_o_fox, "w_o_moba": w_o_moba, "w_out": w_out,
            "norm_ffn": norm_ffn, "w_gate_up": w_gate_up, "w_down": w_down,
            "norm_final": norm_final}

def reference(x, norm_mix, w_in, b_forget, w_o_fox, w_o_moba, w_out,
              norm_ffn, w_gate_up, w_down, norm_final):
    offs = split_offsets()
    for layer in range(DEPTH):
        h = rms_norm(x, norm_mix[layer])
        proj = h @ w_in[layer]
        q_a, k_a, v_a, q_b, k_b, v_b, f_logit, g_a, g_b = jnp.split(proj, offs, axis=-1)
        log_f = jax.nn.log_sigmoid(
            (f_logit + b_forget[layer]).astype(jnp.float32)).transpose(0, 2, 1)
        o_a = forgetting_attention(to_heads(q_a, N_HEADS_FOX), to_heads(k_a, N_HEADS_FOX),
                                   to_heads(v_a, N_HEADS_FOX), log_f)
        o_b = moba_attention(rotary(to_heads(q_b, N_HEADS_MOBA)),
                             rotary(to_heads(k_b, N_HEADS_MOBA)),
                             to_heads(v_b, N_HEADS_MOBA))
        y = (jax.nn.sigmoid(g_a) * (from_heads(o_a) @ w_o_fox[layer])
             + jax.nn.sigmoid(g_b) * (from_heads(o_b) @ w_o_moba[layer]))
        x = x + y @ w_out[layer]
        h = rms_norm(x, norm_ffn[layer])
        gate, up = jnp.split(h @ w_gate_up[layer], [D_FF], axis=-1)
        x = x + (jax.nn.silu(gate) * up) @ w_down[layer]
    return rms_norm(x, norm_final)


_drawn_inputs = setup_inputs


def setup_inputs(seed=0):
    import zlib

    import numpy as np

    out = dict(_drawn_inputs(seed))
    spreads = {}
    factors = {'norm_mix': 7.118, 'norm_ffn': 3.903, 'norm_final': 2.864}
    for name, (base, spread) in spreads.items():
        noise = np.random.default_rng([zlib.crc32(name.encode()), seed]).standard_normal(out[name].shape)
        drawn = base * np.exp(spread * noise) if base else spread * noise
        out[name] = __import__('jax').numpy.asarray(drawn.astype(out[name].dtype))
    for name, factor in factors.items():
        out[name] = (out[name] * factor).astype(out[name].dtype)
    return out
```

```python
from contextlib import ExitStack

import concourse.bass as bass
from concourse import mybir

F32 = mybir.dt.float32
F32R = mybir.dt.float32r
ALU = mybir.AluOpType
ACT = mybir.ActivationFunctionType
AX = mybir.AxisListType

P = 128
TOKENS = 256
TT = TOKENS // P
D = 2048
HEAD = 128
HEADS = 8
WIDTH = HEADS * HEAD
D_FF = 5632
EPS = 1e-6
SCALE = float(HEAD) ** -0.5
MASKED = -1e30

COLS = 512
CHUNK_KT = 2
RING = 4
KT = D // P
FF_KT = D_FF // P
BLOCK_KT = COLS // P
IN_STEPS = KT // CHUNK_KT
O_STEPS = HEADS // CHUNK_KT
FF_STEPS = FF_KT // CHUNK_KT
GROUP_HEADS = COLS // HEAD
HALVES = HEADS // GROUP_HEADS
OUT_GROUPS = D // COLS
FF_GROUPS = D_FF // COLS

K_G, Q_G, V_G, GATE0_G, GATE1_G = range(5)
HALF_STEPS = 5 * IN_STEPS
TURN_QK, SCORES, TURN_P, VALUES, HEAD_STEPS = 18, 19, 22, 26, 4

PASSES = 2 * HALVES
C_MERGE = PASSES * HALF_STEPS
C_OUT = C_MERGE + OUT_GROUPS * 2 * O_STEPS
C_FF = C_OUT + OUT_GROUPS * IN_STEPS
C_DOWN = C_FF + FF_GROUPS * 2 * IN_STEPS
CHUNKS = C_DOWN + OUT_GROUPS * FF_STEPS
PAIR_G = {K_G: (0, 3, 0), Q_G: (1, 2, 0), V_G: (0, 3, 1), GATE0_G: (1, 2, 1), GATE1_G: (0, 3, 2)}
U_MERGE = (3 * PASSES, 2 * PASSES)
U_OUT = (U_MERGE[0] + OUT_GROUPS, U_MERGE[1] + OUT_GROUPS)
U_FF = (U_OUT[0] + OUT_GROUPS // 2, U_OUT[1] + OUT_GROUPS // 2)
U_DOWN = (U_FF[0] + FF_GROUPS, U_FF[1] + FF_GROUPS)
B_MERGE, B_OUT, B_FF = 0, OUT_GROUPS, 2 * OUT_GROUPS


class Chunk:

    def __init__(self, i, per, base):
        self.number = i * per + base
        self.slot = base % RING
        self.use = i * (per // RING) + base // RING
        self.early = isinstance(self.number, int) and self.number < RING


def columns(i, start=0):
    return bass.ds(i * COLS + start, COLS)


def build(nc, x, norm_mix, w_in, b_forget, w_o_fox, w_o_moba, w_out, norm_ffn, w_gate_up, w_down,
          norm_final, rope_cos, rope_sin, out):
    x_rows = x.rearrange("b (t p) n -> p (b t) n", p=P)
    out_rows = out.rearrange("b (t p) n -> p (b t) n", p=P)

    def chunked(w):
        return w.rearrange("l (c k p) n -> (l c) p k n", p=P, k=CHUNK_KT)

    w_in_c, w_fox_c, w_moba_c, w_out_c = chunked(w_in), chunked(w_o_fox), chunked(w_o_moba), chunked(w_out)
    w_ff_c, w_down_c = chunked(w_gate_up), chunked(w_down)
    F_COL = 3 * WIDTH * 2
    GATE_COL = F_COL + HEADS

    with ExitStack() as ctx:
        sem = lambda name: ctx.enter_context(nc.semaphore(name))
        psum = lambda name, shape: ctx.enter_context(nc.psum_tensor(name, shape, F32))

        base = (nc.sbuf_base + 63) // 64 * 64
        at = [base]

        def place(name, shape, dtype=F32, offset=None):
            size = 4
            for n in shape[1:]:
                size *= n
            size = (size + 31) // 32 * 32
            if offset is None:
                offset = at[0]
                at[0] += size
            t = nc.alloc_sbuf_tensor_at(name, shape, dtype, offset=offset)
            return t, offset + size

        weight_raw, _ = place("weight_raw", [P, RING, CHUNK_KT, COLS])
        weight_high, _ = place("weight_high", [P, RING, CHUNK_KT, COLS], F32R)
        weight_low, _ = place("weight_low", [P, RING, CHUNK_KT, COLS], F32R)
        rows, _ = place("rows", [P, TT, D])
        second = at[0]
        o_high, _ = place("o_high", [P, 2 * HEADS, TOKENS], F32R)
        o_low, _ = place("o_low", [P, 2 * HEADS, TOKENS], F32R)
        x2_high, end = place("x2_high", [P, KT, TOKENS], F32R, offset=second)
        x2_low, end = place("x2_low", [P, KT, TOKENS], F32R, offset=end)
        scaled_rows, end = place("scaled_rows", [P, TT, D], offset=second)
        first = at[0]
        x_high, _ = place("x_high", [P, KT, TOKENS], F32R)
        x_low, _ = place("x_low", [P, KT, TOKENS], F32R)
        y_high, end = place("y_high", [P, KT, TOKENS], F32R, offset=first)
        y_low, end = place("y_low", [P, KT, TOKENS], F32R, offset=end)
        gates, _ = place("gates", [P, 2, TT, D])
        k_rows, _ = place("k_rows", [P, TT, COLS])
        q_rows, _ = place("q_rows", [P, TT, COLS])
        v_rows, _ = place("v_rows", [P, TT, COLS])
        rope_a, _ = place("rope_a", [P, TT, COLS])
        rope_b, _ = place("rope_b", [P, TT, COLS])
        qk_turned, _ = place("qk_turned", [P, 2, TOKENS])
        logits, _ = place("logits", [P, 3 * P])
        probs, _ = place("probs", [P, 3 * P])
        probs_turned, _ = place("probs_turned", [P, 3 * P])
        h_high, end = place("h_high", [P, FF_KT, TOKENS], F32R, offset=first)
        h_low, end = place("h_low", [P, FF_KT, TOKENS], F32R, offset=end)
        at[0] = max(at[0], end)
        merge_a, end = place("merge_a", [P, TT, COLS], offset=at[0])
        at[0] = end
        merge_b, end = place("merge_b", [P, TT, COLS], offset=at[0])
        at[0] = end
        identity, _ = place("identity", [P, P])
        causal, _ = place("causal", [P, 3 * P])
        up_to, _ = place("up_to", [P, 2 * P], F32R)
        gain_rows, _ = place("gain_rows", [KT, 2, P])
        gains, _ = place("gains", [P, 2, KT])
        w_forget, _ = place("w_forget", [P, KT, HEADS])
        w_forget_high, _ = place("w_forget_high", [P, KT, HEADS], F32R)
        w_forget_low, _ = place("w_forget_low", [P, KT, HEADS], F32R)
        bias_forget, _ = place("bias_forget", [P, HEADS])
        rope, _ = place("rope", [P, 2, TT, HEAD // 2])
        rope_kq, _ = place("rope_kq", [P, 2, 2, TT, HEAD // 2])
        forget, _ = place("forget", [P, 5, TT, HEADS])
        decay_rows, _ = place("decay_rows", [P, TT, HEADS])
        decay_high, _ = place("decay_high", [P, TT, GROUP_HEADS], F32R)
        decay_low, _ = place("decay_low", [P, TT, GROUP_HEADS], F32R)
        decay_sum, _ = place("decay_sum", [P, TT, GROUP_HEADS])
        squares, _ = place("squares", [P, 3, TT, OUT_GROUPS])
        mean_square, _ = place("mean_square", [P, 3, TT])
        norm_tmp, _ = place("norm_tmp", [P, 3, 6, TT])
        rstd, _ = place("rstd", [P, 3, TT])
        rstd_neg, _ = place("rstd_neg", [P, 3, TT])
        rstd_q, _ = place("rstd_q", [P, TT])
        row_max_neg, _ = place("row_max_neg", [P, TT])
        row_sum, _ = place("row_sum", [P, TT])
        row_sum_inv, _ = place("row_sum_inv", [P, TT])
        ones, _ = place("ones", [P, 2 * P])
        merge = (merge_a, merge_b)
        merge_y, silu, hidden_rows = k_rows, merge_a, merge_b
        final_gain, _ = place("final_gain", [P, D], offset=second + 4 * TT * D)

        acc = [psum(f"acc{n}", [P, TT, COLS]) for n in range(2)]
        turn = psum("turn", [P, 2, COLS])
        turn2 = psum("turn2", [P, 2, COLS])
        ps_qk, ps_scores, ps_probs, ps_o = turn[:, 0, :], turn[:, 1, :], turn2[:, 0, :], turn2[:, 1, :]
        ps_forget = acc[1][:, 0, 0:TT * HEADS].rearrange("p (t h) -> p t h", t=TT)
        ps_gain = acc[1][:, 1, 0:2 * KT].rearrange("p (g k) -> p g k", g=2)

        x_landed, small_landed, wf_landed, gain_landed, fin_landed = map(
            sem, ("x_landed", "small_landed", "wf_landed", "gain_landed", "fin_landed"))
        stored = sem("stored")
        raw_landed = [sem(f"raw_landed{n}") for n in range(RING)]
        raw_free = sem("raw_free")
        high_ready = sem("high_ready")
        chunk_used = sem("chunk_used")
        evacuated = [sem(f"evacuated{n}") for n in range(2)]
        zeroed, consts = sem("zeroed"), sem("consts")
        gains_turned, gains_ready = sem("gains_turned"), sem("gains_ready")
        x_turned, x_rounded, x_split = sem("x_turned"), sem("x_rounded"), sem("x_split")
        wf_rounded, wf_split = sem("wf_rounded"), sem("wf_split")
        forget_logits = sem("forget_logits")
        squares_ready = sem("squares_ready")
        norm_vec, norm_act = sem("norm_vec"), sem("norm_act")
        squares_summed, rstd_ready, rstd_q_ready = sem("squares_summed"), sem("rstd_ready"), sem("rstd_q_ready")
        forget_vec, forget_act = sem("forget_vec"), sem("forget_act")
        decay_rounded, decay_split = sem("decay_rounded"), sem("decay_split")
        decay_summed, decay_ready = sem("decay_summed"), sem("decay_ready")
        rope_vec = sem("rope_vec")
        qk_in_psum, qk_copied = sem("qk_in_psum"), sem("qk_copied")
        scores_in_psum, scores_masked = sem("scores_in_psum"), sem("scores_masked")
        row_max_ready, exp_done = sem("row_max_ready"), sem("exp_done")
        row_sum_inverted, probs_ready = sem("row_sum_inverted"), sem("probs_ready")
        probs_in_psum, probs_copied = sem("probs_in_psum"), sem("probs_copied")
        o_in_psum, o_rounded, o_split = sem("o_in_psum"), sem("o_rounded"), sem("o_split")
        gate_ready = sem("gate_ready")
        merged = sem("merged")
        block_turned, block_rounded, block_split = sem("block_turned"), sem("block_rounded"), sem("block_split")
        final_scaled, result_ready = sem("final_scaled"), sem("result_ready")

        def split_count(chunk):
            return chunk.number + RING + 1

        def pair_use(g, it):
            pair, per, n = PAIR_G[g]
            return pair, it * per + n

        block = ctx.enter_context(nc.Block())

        @block.sync
        def _(sp):
            for t in range(TT):
                sp.dma_start(rows[:, t, :], x_rows[:, t, :]).then_inc(x_landed, 16)
            sp.sem_inc(raw_free, RING)

            def load(chunk, source):
                sp.wait_ge(raw_free, chunk.number + 1)
                sp.dma_start(weight_raw[:, chunk.slot, :, :], source).then_inc(raw_landed[chunk.slot], 16)

            for branch in range(2):
                with sp.Fori(1, HALVES + 1) as half_1:
                    at0 = 3 * WIDTH * branch
                    gate = GATE_COL + D * branch
                    first_col = [half_1 * COLS + (at0 + WIDTH - COLS), half_1 * COLS + (at0 - COLS),
                                 half_1 * COLS + (at0 + 2 * WIDTH - COLS),
                                 half_1 * (2 * COLS) + (gate - 2 * COLS), half_1 * (2 * COLS) + (gate - COLS)]
                    for g in range(5):
                        for c in range(IN_STEPS):
                            load(Chunk(half_1 - 1, HALF_STEPS, HALVES * branch * HALF_STEPS + g * IN_STEPS + c),
                                 w_in_c[c][:, :, bass.ds(first_col[g], COLS)])
            with sp.Fori(1, OUT_GROUPS + 1) as n_1:
                for c in range(2 * O_STEPS):
                    w = w_fox_c if c < O_STEPS else w_moba_c
                    load(Chunk(n_1 - 1, 2 * O_STEPS, C_MERGE + c), w[c % O_STEPS][:, :, columns(n_1, -COLS)])
            with sp.Fori(1, OUT_GROUPS + 1) as n_1:
                for c in range(IN_STEPS):
                    load(Chunk(n_1 - 1, IN_STEPS, C_OUT + c), w_out_c[c][:, :, columns(n_1, -COLS)])
            with sp.Fori(1, FF_GROUPS + 1) as n_1:
                for c in range(2 * IN_STEPS):
                    load(Chunk(n_1 - 1, 2 * IN_STEPS, C_FF + c),
                         w_ff_c[c % IN_STEPS][:, :, columns(n_1, D_FF * (c // IN_STEPS) - COLS)])
            with sp.Fori(1, OUT_GROUPS // 2 + 1) as i_1:
                for c in range(2 * FF_STEPS):
                    load(Chunk(i_1 - 1, 2 * FF_STEPS, C_DOWN + c),
                         w_down_c[c % FF_STEPS][:, :, bass.ds(i_1 * (2 * COLS) + COLS * (c // FF_STEPS - 2), COLS)])
            for t in range(TT):
                sp.wait_ge(result_ready, t + 1)
                sp.dma_start(out_rows[:, t, :], scaled_rows[:, t, :]).then_inc(stored, 16)
            sp.wait_ge(stored, 16 * TT)

        @block.gpsimd
        def _(pool):
            pool.memset(identity[:, :], 0.0).then_inc(zeroed, 1)
            pool.memset(causal[:, :], 0.0).then_inc(zeroed, 1)
            pool.memset(ones[:, 0:2 * P], 1.0).then_inc(zeroed, 1)
            pool.wait_ge(zeroed, 3)
            pool.affine_select(out=identity[:, :], in_=identity[:, :], compare_op=ALU.not_equal, fill=1.0,
                               base=0, pattern=[[-1, P]], channel_multiplier=1).then_inc(consts, 1)
            for n in (0, 2):
                own = causal[:, n * P:(n + 1) * P]
                pool.affine_select(out=own, in_=own, compare_op=ALU.is_ge, fill=MASKED,
                                   base=0, pattern=[[-1, P]], channel_multiplier=1).then_inc(consts, 1)
            pool.affine_select(out=ones[:, 0:P], in_=ones[:, 0:P], compare_op=ALU.is_ge, fill=0.0,
                               base=0, pattern=[[1, P]], channel_multiplier=-1).then_inc(consts, 1)
            pool.wait_ge(consts, 4)
            pool.tensor_copy(up_to[:, :], ones[:, 0:2 * P]).then_inc(consts, 1)

        @block.scalar
        def _(act):
            for n, g in enumerate((norm_mix, norm_ffn)):
                act.dma_start(gain_rows[:, n, :], g.rearrange("l (k p) -> (l k) p", p=P))\
                   .then_inc(gain_landed, 16)
            act.dma_start(bias_forget[:, :], b_forget.broadcast_to([P, HEADS])).then_inc(small_landed, 16)
            for n, table in enumerate((rope_cos, rope_sin)):
                act.dma_start(rope[:, n, :, :], table.rearrange("(t p) d -> p t d", p=P))\
                   .then_inc(small_landed, 16)
            act.dma_start(w_forget[:, :, :], w_in.rearrange("l (k p) n -> p (l k) n", p=P)[:, :, F_COL:GATE_COL])\
               .then_inc(wf_landed, 16)

            def round_chunk(chunk):
                act.wait_ge(raw_landed[chunk.slot], chunk.use * 16 + 16)
                if not chunk.early:
                    act.wait_ge(chunk_used, chunk.number - RING + 1)
                act.activation(weight_high[:, chunk.slot, :, :], weight_raw[:, chunk.slot, :, :], ACT.Copy)\
                   .then_inc(high_ready, 1)

            def round_block(dst, kt, scales, number):
                act.wait_ge(block_turned, number + 1)
                if scales is None:
                    act.activation(dst[:, bass.ds(kt, BLOCK_KT), :],
                                   turn[:, :, :].rearrange("p a (j n) -> p (a j) n", n=TOKENS), ACT.Copy)\
                       .then_inc(block_rounded, 1)
                    return
                for j in range(BLOCK_KT):
                    last = act.activation(dst[:, kt + j, :], turn[:, j // 2, (j % 2) * TOKENS:(j % 2 + 1) * TOKENS],
                                          ACT.Copy, scale=scales[:, kt + j:kt + j + 1])
                last.then_inc(block_rounded, 1)

            def root(n):
                act.wait_ge(norm_vec, 5 * n + 1)
                act.activation(norm_tmp[:, n, 0, :], mean_square[:, n, :], ACT.Ln).then_inc(norm_act, 1)
                act.wait_ge(norm_act, 2 * n + 1)
                act.activation(norm_tmp[:, n, 1, :], norm_tmp[:, n, 0, :], ACT.Exp, scale=-0.5)\
                   .then_inc(norm_act, 1)

            act.wait_ge(gains_ready, 1)
            for b in range(KT // BLOCK_KT):
                act.wait_ge(x_turned, b + 1)
                pair = (turn, turn2)[b % 2]
                for j in range(BLOCK_KT):
                    kt = b * BLOCK_KT + j
                    last = act.activation(x_high[:, kt, :], pair[:, j // 2, (j % 2) * TOKENS:(j % 2 + 1) * TOKENS],
                                          ACT.Copy, scale=gains[:, 0, kt:kt + 1])
                last.then_inc(x_rounded, 1)
                round_chunk(Chunk(0, RING, b))
            act.wait_ge(wf_landed, 16)
            act.activation(w_forget_high[:, :, :], w_forget[:, :, :], ACT.Copy).then_inc(wf_rounded, 1)
            act.wait_ge(x_landed, 16 * TT)
            for t in range(TT):
                last = act.activation(gates[:, 0, t, :], rows[:, t, :], ACT.Square, accum_out=squares[:, 0, t, 0:1])
            last.then_inc(squares_ready, 1)
            root(0)
            act.wait_ge(forget_vec, 4)
            act.activation(forget[:, 3, :, :], forget[:, 1, :, :], ACT.Exp, scale=-1.0).then_inc(forget_act, 1)
            act.wait_ge(forget_act, 1)
            act.activation(forget[:, 4, :, :], forget[:, 3, :, :], ACT.Ln, bias=1.0).then_inc(forget_act, 1)
            act.wait_ge(rstd_ready, 1)

            def take_out(dst, g, it, half, branch, scales):
                pair, use = pair_use(g, it)
                act.wait_ge(chunk_used, Chunk(half, HALF_STEPS, HALVES * branch * HALF_STEPS
                                              + (g + 1) * IN_STEPS - 1).number + 1)
                for t in range(TT):
                    last = act.activation(dst[:, t, :], acc[pair][:, t, :], ACT.Copy, scale=scales[:, t:t + 1])
                last.then_inc(evacuated[pair], 1)

            def take_out_gate(g, it, half, branch):
                pair, _ = pair_use(g, it)
                act.wait_ge(chunk_used, Chunk(half, HALF_STEPS, HALVES * branch * HALF_STEPS
                                              + (g + 1) * IN_STEPS - 1).number + 1)
                for t in range(TT):
                    last = act.activation(gates[:, branch, t, bass.ds(half * 2 * COLS + COLS * (g - GATE0_G), COLS)],
                                          acc[pair][:, t, :], ACT.Copy, scale=rstd[:, 0, t:t + 1])
                last.then_inc(evacuated[pair], 1)

            for branch in range(2):
                with act.Fori(0, HALVES) as half:
                    it = half + HALVES * branch
                    for s in range(HALF_STEPS):
                        if branch == 0 and s == IN_STEPS - 1:
                            take_out(k_rows, K_G, it, half, branch, rstd[:, 0, :])
                        if branch == 0 and s == 2 * IN_STEPS - 1:
                            take_out(q_rows, Q_G, it, half, branch, rstd_q)
                        if s == 3 * IN_STEPS - 1:
                            take_out(v_rows, V_G, it, half, branch, rstd[:, 0, :])
                        if s == 4 * IN_STEPS - 1:
                            take_out_gate(GATE0_G, it, half, branch)
                        for h in range(GROUP_HEADS):
                            head = it * GROUP_HEADS + h
                            at_step = s - HEAD_STEPS * h
                            if at_step == VALUES:
                                act.wait_ge(o_in_psum, head + 1)
                                act.activation(o_high[:, bass.ds(head, 1), :],
                                               ps_o[:, 0:TOKENS].unsqueeze(1), ACT.Copy).then_inc(o_rounded, 1)
                            if at_step == TURN_QK:
                                act.wait_ge(qk_in_psum, head + 1)
                                act.activation(qk_turned[:, :, :].rearrange("p a n -> p (a n)"), ps_qk, ACT.Copy)\
                                   .then_inc(qk_copied, 1)
                            if at_step == SCORES:
                                act.wait_ge(row_max_ready, head + 1)
                                act.activation(probs[:, 0:P], logits[:, 0:P], ACT.Exp,
                                               bias=row_max_neg[:, 0:1], accum_out=row_sum[:, 0:1])
                                act.activation(probs[:, P:3 * P], logits[:, P:3 * P], ACT.Exp,
                                               bias=row_max_neg[:, 1:2], accum_out=row_sum[:, 1:2])\
                                   .then_inc(exp_done, 1)
                            if at_step == TURN_P:
                                act.wait_ge(probs_in_psum, head + 1)
                                act.activation(probs_turned[:, :], ps_probs[:, 0:3 * P], ACT.Copy)\
                                   .then_inc(probs_copied, 1)
                        if s == HALF_STEPS - 1:
                            take_out_gate(GATE1_G, it, half, branch)
                        round_chunk(Chunk(half, HALF_STEPS, HALVES * branch * HALF_STEPS + s + RING))

            def merge_steps(n, first):
                for s in range(2 * O_STEPS):
                    if s % O_STEPS == 0:
                        branch = s // O_STEPS
                        if not first and s == 0:
                            act.wait_ge(merged, n)
                        act.activation(merge[branch][:, :, :], gates[:, branch, :, columns(n)], ACT.Sigmoid)\
                           .then_inc(gate_ready, 1)
                    if s == 2 and not first:
                        round_block(y_high, (n - 1) * BLOCK_KT, None, n + B_MERGE - 1)
                    round_chunk(Chunk(n, 2 * O_STEPS, C_MERGE + s + RING))

            merge_steps(0, True)
            with act.Fori(1, OUT_GROUPS) as n:
                merge_steps(n, False)

            def sum_squares(norm, n, pair, use):
                act.wait_ge(evacuated[pair], use + 1)
                for t in range(TT):
                    last = act.activation(merge_a[:, t, :], rows[:, t, n * COLS:(n + 1) * COLS], ACT.Square,
                                          accum_out=squares[:, norm, t, n:n + 1])
                if n == OUT_GROUPS - 1:
                    last.then_inc(squares_ready, 1)

            for n in range(OUT_GROUPS):
                for s in range(IN_STEPS):
                    if s == 2:
                        if n == 0:
                            round_block(y_high, (OUT_GROUPS - 1) * BLOCK_KT, None, B_OUT - 1)
                        else:
                            round_block(x2_high, (n - 1) * BLOCK_KT, gains[:, 1, :], B_OUT + n - 1)
                    if s == IN_STEPS - 1:
                        sum_squares(1, n, n % 2, U_OUT[n % 2] + n // 2)
                    round_chunk(Chunk(n, IN_STEPS, C_OUT + s + RING))

            def ff_steps(n, first):
                for s in range(2 * IN_STEPS):
                    if s == 0 and first:
                        root(1)
                    if s == 2:
                        if first:
                            round_block(x2_high, (OUT_GROUPS - 1) * BLOCK_KT, gains[:, 1, :], B_FF - 1)
                        else:
                            round_block(h_high, (n - 1) * BLOCK_KT, None, n + B_FF - 1)
                    if s == IN_STEPS - 1:
                        if first:
                            act.wait_ge(rstd_ready, 2)
                        act.wait_ge(chunk_used, Chunk(n, 2 * IN_STEPS, C_FF + s).number + 1)
                        for t in range(TT):
                            last = act.activation(silu[:, t, :], acc[0][:, t, :], ACT.Silu,
                                                  scale=rstd[:, 1, t:t + 1])
                        last.then_inc(evacuated[0], 1)
                    round_chunk(Chunk(n, 2 * IN_STEPS, C_FF + s + RING))

            ff_steps(0, True)
            with act.Fori(1, FF_GROUPS) as n:
                ff_steps(n, False)
            round_block(h_high, (FF_GROUPS - 1) * BLOCK_KT, None, B_FF + FF_GROUPS - 1)

            act.wait_ge(chunk_used, C_DOWN)
            act.dma_start(final_gain[:, :], norm_final.rearrange("(a n) -> a n", a=1).broadcast_to([P, D]))\
               .then_inc(fin_landed, 16)
            for n in range(OUT_GROUPS):
                for s in range(FF_STEPS):
                    if s == FF_STEPS - 1:
                        sum_squares(2, n, n % 2, U_DOWN[n % 2] + n // 2)
                    if C_DOWN + n * FF_STEPS + s + RING < CHUNKS:
                        round_chunk(Chunk(0, RING, C_DOWN + n * FF_STEPS + s + RING))
            root(2)
            act.wait_ge(rstd_ready, 3)
            act.wait_ge(final_scaled, OUT_GROUPS)
            act.activation(scaled_rows[:, 0, :], scaled_rows[:, 0, :], ACT.Copy, scale=rstd[:, 2, 0:1])\
               .then_inc(result_ready, 1)

        @block.vector
        def _(dve):
            def rest_of_chunk(chunk):
                dve.wait_ge(high_ready, chunk.number + 1)
                dve.tensor_tensor(weight_low[:, chunk.slot, :, :], weight_raw[:, chunk.slot, :, :],
                                  weight_high[:, chunk.slot, :, :].bitcast(F32), ALU.subtract)\
                   .then_inc(raw_free, 1)

            def rest_of_block(high, low, kt, scales, number):
                dve.wait_ge(block_rounded, number + 1)
                if scales is None:
                    dve.tensor_tensor(low[:, bass.ds(kt, BLOCK_KT), :],
                                      turn[:, :, :].rearrange("p a (j n) -> p (a j) n", n=TOKENS),
                                      high[:, bass.ds(kt, BLOCK_KT), :].bitcast(F32), ALU.subtract)\
                       .then_inc(block_split, 1)
                    return
                for j in range(BLOCK_KT):
                    last = dve.scalar_tensor_tensor(
                        out=low[:, kt + j, :], in0=turn[:, j // 2, (j % 2) * TOKENS:(j % 2 + 1) * TOKENS],
                        scalar=scales[:, kt + j:kt + j + 1], in1=high[:, kt + j, :].bitcast(F32),
                        op0=ALU.mult, op1=ALU.subtract)
                last.then_inc(block_split, 1)

            def root(n):
                v, y0 = mean_square[:, n, :], norm_tmp[:, n, 1, :]
                t1, t2, t3, total = (norm_tmp[:, n, 2 + k, :] for k in range(4))
                dve.wait_ge(squares_ready, n + 1)
                dve.tensor_reduce(total, squares[:, n, :, 0:OUT_GROUPS if n else 1], AX.X, ALU.add).then_inc(squares_summed, 1)
                dve.wait_ge(squares_summed, n + 1)
                dve.tensor_scalar(v, total, 1.0 / D, EPS, ALU.mult, ALU.add).then_inc(norm_vec, 1)
                dve.wait_ge(norm_act, 2 * n + 2)
                dve.tensor_tensor(t1, y0, y0, ALU.mult).then_inc(norm_vec, 1)
                dve.wait_ge(norm_vec, 5 * n + 2)
                dve.tensor_tensor(t2, t1, v, ALU.mult).then_inc(norm_vec, 1)
                dve.wait_ge(norm_vec, 5 * n + 3)
                dve.tensor_scalar(t3, t2, -0.5, 1.5, ALU.mult, ALU.add).then_inc(norm_vec, 1)
                dve.wait_ge(norm_vec, 5 * n + 4)
                dve.tensor_tensor(rstd[:, n, :], y0, t3, ALU.mult).then_inc(norm_vec, 1)
                dve.wait_ge(norm_vec, 5 * n + 5)
                dve.tensor_scalar(rstd_neg[:, n, :], rstd[:, n, :], -1.0, None, ALU.mult).then_inc(rstd_ready, 1)

            dve.wait_ge(gains_turned, 1)
            dve.tensor_copy(gains[:, :, :], ps_gain).then_inc(gains_ready, 1)
            dve.wait_ge(gains_ready, 1)
            for b in range(KT // BLOCK_KT):
                dve.wait_ge(x_rounded, b + 1)
                pair = (turn, turn2)[b % 2]
                for j in range(BLOCK_KT):
                    kt = b * BLOCK_KT + j
                    last = dve.scalar_tensor_tensor(
                        out=x_low[:, kt, :], in0=pair[:, j // 2, (j % 2) * TOKENS:(j % 2 + 1) * TOKENS],
                        scalar=gains[:, 0, kt:kt + 1], in1=x_high[:, kt, :].bitcast(F32),
                        op0=ALU.mult, op1=ALU.subtract)
                last.then_inc(x_split, 1)
                rest_of_chunk(Chunk(0, RING, b))
            dve.wait_ge(wf_rounded, 1)
            dve.tensor_tensor(w_forget_low[:, :, :], w_forget[:, :, :], w_forget_high[:, :, :].bitcast(F32),
                              ALU.subtract).then_inc(wf_split, 1)
            root(0)
            dve.tensor_scalar(rstd_q[:, :], rstd[:, 0, :], SCALE, None, ALU.mult).then_inc(rstd_q_ready, 1)
            dve.wait_ge(rstd_q_ready, 1)
            dve.wait_ge(forget_logits, 1)
            dve.wait_ge(small_landed, 48)
            for t in range(TT):
                dve.scalar_tensor_tensor(out=forget[:, 0, t, :], in0=ps_forget[:, t, :], scalar=rstd[:, 0, t:t + 1],
                                         in1=bias_forget[:, :], op0=ALU.mult, op1=ALU.add).then_inc(forget_vec, 1)
            dve.wait_ge(forget_vec, 2)
            dve.tensor_scalar(forget[:, 2, :, :], forget[:, 0, :, :], -1.0, None, ALU.mult).then_inc(forget_vec, 1)
            dve.wait_ge(forget_vec, 3)
            dve.tensor_tensor(forget[:, 1, :, :], forget[:, 0, :, :], forget[:, 2, :, :], ALU.max)\
               .then_inc(forget_vec, 1)
            dve.wait_ge(forget_act, 2)
            dve.scalar_tensor_tensor(out=decay_rows[:, :, :].rearrange("p t h -> p (t h)"),
                                     in0=forget[:, 2, :, :].rearrange("p t h -> p (t h)"), scalar=0.0,
                                     in1=forget[:, 4, :, :].rearrange("p t h -> p (t h)"),
                                     op0=ALU.max, op1=ALU.add).then_inc(forget_vec, 1)
            for kq in range(2):
                for t in range(TT):
                    for cs in range(2):
                        scale = rstd[:, 0, t:t + 1] if kq == 0 else rstd_q[:, t:t + 1]
                        dve.tensor_scalar(rope_kq[:, kq, cs, t, :], rope[:, cs, t, :], scale, None, ALU.mult)\
                           .then_inc(rope_vec, 1)
            dve.wait_ge(forget_vec, 5)
            dve.wait_ge(rope_vec, 8)

            def rotate(dst, g, it, half, branch, kq, turn_no):
                pair, use = pair_use(g, it)
                dve.wait_ge(chunk_used, Chunk(half, HALF_STEPS, HALVES * branch * HALF_STEPS
                                              + (g + 1) * IN_STEPS - 1).number + 1)
                src = acc[pair][:, :, :].rearrange("p t (e d) -> p t e d", d=HEAD // 2)
                for cs, tmp in ((0, rope_a), (1, rope_b)):
                    table = rope_kq[:, kq, cs, :, :].unsqueeze(2).broadcast_to([P, TT, COLS // (HEAD // 2), HEAD // 2])
                    dve.tensor_tensor(tmp[:, :, :].rearrange("p t (e d) -> p t e d", d=HEAD // 2), src, table,
                                      ALU.mult).then_inc(rope_vec, 1)
                done = half * 6 + 8 + 3 * turn_no
                dve.wait_ge(rope_vec, done + 2)
                halves = lambda a: a[:, :, :].rearrange("p t (h e d) -> p (t h) e d", e=2, d=HEAD // 2)
                o, a, b = halves(dst), halves(rope_a), halves(rope_b)
                dve.tensor_tensor(o[:, :, 0, :], a[:, :, 0, :], b[:, :, 1, :], ALU.subtract).then_inc(rope_vec, 1)
                dve.tensor_tensor(o[:, :, 1, :], a[:, :, 1, :], b[:, :, 0, :], ALU.add).then_inc(evacuated[pair], 1)

            for branch in range(2):
                with dve.Fori(0, HALVES) as half:
                    it = half + HALVES * branch
                    for s in range(HALF_STEPS):
                        if branch == 0 and s == 0:
                            dve.tensor_copy(decay_high[:, :, :], decay_rows[:, :, bass.ds(half * GROUP_HEADS, GROUP_HEADS)])\
                               .then_inc(decay_rounded, 1)
                            dve.wait_ge(decay_rounded, it + 1)
                            dve.tensor_tensor(decay_low[:, :, :], decay_rows[:, :, bass.ds(half * GROUP_HEADS, GROUP_HEADS)],
                                              decay_high[:, :, :].bitcast(F32), ALU.subtract).then_inc(decay_split, 1)
                        if branch == 0 and s == IN_STEPS:
                            dve.wait_ge(decay_summed, it + 1)
                            dve.tensor_scalar(decay_sum[:, :, :], ps_probs[:, 0:TT * GROUP_HEADS]
                                              .rearrange("p (t h) -> p t h", t=TT), -1.0, None, ALU.mult)\
                               .then_inc(decay_ready, 1)
                            dve.wait_ge(decay_ready, it + 1)
                        if branch == 1 and s == IN_STEPS - 1:
                            rotate(k_rows, K_G, it, half, branch, 0, 0)
                        if branch == 1 and s == 2 * IN_STEPS - 1:
                            rotate(q_rows, Q_G, it, half, branch, 1, 1)
                        for h in range(GROUP_HEADS):
                            head = it * GROUP_HEADS + h
                            at_step = s - HEAD_STEPS * h
                            if at_step == VALUES:
                                dve.wait_ge(o_rounded, head + 1)
                                dve.tensor_tensor(o_low[:, bass.ds(head, 1), :], ps_o[:, 0:TOKENS].unsqueeze(1),
                                                  o_high[:, bass.ds(head, 1), :].bitcast(F32), ALU.subtract)\
                                   .then_inc(o_split, 1)
                            if at_step == SCORES:
                                dve.wait_ge(scores_in_psum, head + 1)
                                if branch == 0:
                                    for t, (a, b) in enumerate(((0, P), (P, 3 * P))):
                                        last = dve.scalar_tensor_tensor(
                                            out=logits[:, a:b], in0=ps_scores[:, a:b], scalar=decay_sum[:, t, h:h + 1],
                                            in1=causal[:, a:b], op0=ALU.add, op1=ALU.add)
                                    last.then_inc(scores_masked, 1)
                                else:
                                    dve.tensor_tensor(logits[:, :], ps_scores[:, 0:3 * P], causal[:, :], ALU.add)\
                                       .then_inc(scores_masked, 1)
                                dve.wait_ge(scores_masked, head + 1)
                                dve.tensor_reduce(row_max_neg[:, 0:1], logits[:, 0:P], AX.X, ALU.max, negate=True)
                                dve.tensor_reduce(row_max_neg[:, 1:2], logits[:, P:3 * P], AX.X, ALU.max, negate=True)\
                                   .then_inc(row_max_ready, 1)
                            if at_step == SCORES + 1:
                                dve.wait_ge(exp_done, head + 1)
                                dve.reciprocal(row_sum_inv[:, :], row_sum[:, :]).then_inc(row_sum_inverted, 1)
                                dve.wait_ge(row_sum_inverted, head + 1)
                                dve.tensor_scalar(probs[:, 0:P], probs[:, 0:P], row_sum_inv[:, 0:1], None, ALU.mult)
                                dve.tensor_scalar(probs[:, P:3 * P], probs[:, P:3 * P], row_sum_inv[:, 1:2], None,
                                                  ALU.mult).then_inc(probs_ready, 1)
                        rest_of_chunk(Chunk(half, HALF_STEPS, HALVES * branch * HALF_STEPS + s + RING))

            def merge_steps(n, first):
                for s in range(2 * O_STEPS):
                    if s == 2 and not first:
                        rest_of_block(y_high, y_low, (n - 1) * BLOCK_KT, None, n + B_MERGE - 1)
                    for branch, dst in enumerate(merge):
                        if s == (branch + 1) * O_STEPS - 1:
                            dve.wait_ge(chunk_used, Chunk(n, 2 * O_STEPS, C_MERGE + s).number + 1)
                            dve.wait_ge(gate_ready, n * 2 + branch + 1)
                            dve.tensor_tensor(dst[:, :, :], acc[branch][:, :, :], dst[:, :, :], ALU.mult).then_inc(evacuated[branch], 1)
                    if s == 2 * O_STEPS - 1:
                        dve.wait_ge(evacuated[0], n + U_MERGE[0] + 1)
                        dve.wait_ge(evacuated[1], n + U_MERGE[1] + 1)
                        dve.tensor_tensor(merge_y[:, :, :], merge[0][:, :, :], merge[1][:, :, :], ALU.add)\
                           .then_inc(merged, 1)
                    rest_of_chunk(Chunk(n, 2 * O_STEPS, C_MERGE + s + RING))

            merge_steps(0, True)
            with dve.Fori(1, OUT_GROUPS) as n:
                merge_steps(n, False)

            def add_residual(n, pair, last_chunk):
                dve.wait_ge(chunk_used, last_chunk + 1)
                piece = rows[:, :, n * COLS:(n + 1) * COLS]
                dve.tensor_tensor(piece, acc[pair][:, :, :], piece, ALU.add).then_inc(evacuated[pair], 1)

            for n in range(OUT_GROUPS):
                for s in range(IN_STEPS):
                    if s == 2:
                        if n == 0:
                            rest_of_block(y_high, y_low, (OUT_GROUPS - 1) * BLOCK_KT, None, B_OUT - 1)
                        else:
                            rest_of_block(x2_high, x2_low, (n - 1) * BLOCK_KT, gains[:, 1, :], B_OUT + n - 1)
                    if s == IN_STEPS - 1:
                        add_residual(n, n % 2, C_OUT + (n + 1) * IN_STEPS - 1)
                    rest_of_chunk(Chunk(n, IN_STEPS, C_OUT + s + RING))

            def ff_steps(n, first):
                for s in range(2 * IN_STEPS):
                    if s == 0 and first:
                        root(1)
                    if s == 2:
                        if first:
                            rest_of_block(x2_high, x2_low, (OUT_GROUPS - 1) * BLOCK_KT, gains[:, 1, :], B_FF - 1)
                        else:
                            rest_of_block(h_high, h_low, (n - 1) * BLOCK_KT, None, n + B_FF - 1)
                    if s == 2 * IN_STEPS - 1:
                        dve.wait_ge(chunk_used, Chunk(n, 2 * IN_STEPS, C_FF + s).number + 1)
                        dve.wait_ge(evacuated[0], n + U_FF[0] + 1)
                        for t in range(TT):
                            last = dve.scalar_tensor_tensor(out=hidden_rows[:, t, :], in0=acc[1][:, t, :],
                                                            scalar=rstd[:, 1, t:t + 1], in1=silu[:, t, :],
                                                            op0=ALU.mult, op1=ALU.mult)
                        last.then_inc(evacuated[1], 1)
                    rest_of_chunk(Chunk(n, 2 * IN_STEPS, C_FF + s + RING))

            ff_steps(0, True)
            with dve.Fori(1, FF_GROUPS) as n:
                ff_steps(n, False)
            rest_of_block(h_high, h_low, (FF_GROUPS - 1) * BLOCK_KT, None, B_FF + FF_GROUPS - 1)

            dve.wait_ge(fin_landed, 16)
            for n in range(OUT_GROUPS):
                for s in range(FF_STEPS):
                    if s == FF_STEPS - 1:
                        add_residual(n, n % 2, C_DOWN + (n + 1) * FF_STEPS - 1)
                        dve.wait_ge(evacuated[n % 2], U_DOWN[n % 2] + n // 2 + 1)
                        gain = final_gain[:, n * COLS:(n + 1) * COLS].unsqueeze(1).broadcast_to([P, TT, COLS])
                        dve.tensor_tensor(scaled_rows[:, :, n * COLS:(n + 1) * COLS],
                                          rows[:, :, n * COLS:(n + 1) * COLS], gain, ALU.mult)\
                           .then_inc(final_scaled, 1)
                    if C_DOWN + n * FF_STEPS + s + RING < CHUNKS:
                        rest_of_chunk(Chunk(0, RING, C_DOWN + n * FF_STEPS + s + RING))
            root(2)
            dve.wait_ge(final_scaled, OUT_GROUPS)
            dve.wait_ge(result_ready, 1)
            dve.tensor_scalar(scaled_rows[:, 1, :], scaled_rows[:, 1, :], rstd[:, 2, 1:2], None, ALU.mult)\
               .then_inc(result_ready, 1)

        @block.tensor
        def _(pe):
            def multiply(chunk, high, low, kt, pair, first, last):
                pe.wait_ge(raw_free, split_count(chunk))
                for k in range(CHUNK_KT):
                    for t in range(TT):
                        x_h = high[:, kt + k, t * P:(t + 1) * P]
                        x_l = low[:, kt + k, t * P:(t + 1) * P]
                        w_h, w_l = weight_high[:, chunk.slot, k, :], weight_low[:, chunk.slot, k, :]
                        o = acc[pair][:, t, :]
                        pe.matmul(o, x_h, w_h, start=first and k == 0, stop=False)
                        pe.matmul(o, x_h, w_l, start=False, stop=False)
                        mm = pe.matmul(o, x_l, w_h, start=False, stop=last and k == CHUNK_KT - 1)
                mm.then_inc(chunk_used, 1)

            def turn_block(src, pair, what=block_turned):
                for j in range(BLOCK_KT):
                    for t in range(TT):
                        last = pe.transpose(pair[:, j // 2, (j % 2) * TOKENS + t * P:(j % 2) * TOKENS + (t + 1) * P],
                                            src[:, t, j * P:(j + 1) * P], identity[:, :])
                last.then_inc(what, 1)

            pe.wait_ge(consts, 5)
            pe.wait_ge(gain_landed, 32)
            for n in range(2):
                last = pe.transpose(ps_gain[:, n, :], gain_rows[:, n, :], identity[0:KT, 0:KT])
            last.then_inc(gains_turned, 1)
            pe.wait_ge(x_landed, 16 * TT)
            for b in range(KT // BLOCK_KT):
                if b >= 2:
                    pe.wait_ge(x_split, b - 1)
                turn_block(rows[:, :, b * COLS:(b + 1) * COLS], (turn, turn2)[b % 2], x_turned)
            pe.wait_ge(x_split, KT // BLOCK_KT)
            pe.wait_ge(gains_ready, 1)
            pe.wait_ge(wf_split, 1)
            for t in range(TT):
                for kt in range(KT):
                    x_h, x_l = x_high[:, kt, t * P:(t + 1) * P], x_low[:, kt, t * P:(t + 1) * P]
                    pe.matmul(ps_forget[:, t, :], x_h, w_forget_high[:, kt, :], start=kt == 0, stop=False)
                    pe.matmul(ps_forget[:, t, :], x_h, w_forget_low[:, kt, :], start=False, stop=False)
                    last = pe.matmul(ps_forget[:, t, :], x_l, w_forget_high[:, kt, :], start=False, stop=kt == KT - 1)
            last.then_inc(forget_logits, 1)

            def sum_decay(it):
                pe.wait_ge(decay_split, it + 1)
                n = GROUP_HEADS
                terms = [(0, 0, up_to[:, 0:P]), (n, 0, up_to[:, P:2 * P]), (n, 1, up_to[:, 0:P])]
                for k, (o, t, ones) in enumerate(terms):
                    for part in (decay_high, decay_low):
                        last = pe.matmul(ps_probs[:, o:o + n], ones, part[:, t, :],
                                         start=k < 2 and part is decay_high, stop=k != 1 and part is decay_low)
                last.then_inc(decay_summed, 1)

            def turn_qk(it, h, head):
                pair_q, use_q = pair_use(Q_G, it)
                pair_k, use_k = pair_use(K_G, it)
                pe.wait_ge(evacuated[pair_k], use_k + 1)
                pe.wait_ge(evacuated[pair_q], use_q + 1)
                for n, src in enumerate((q_rows, k_rows)):
                    for t in range(TT):
                        last = pe.transpose(ps_qk[:, n * TOKENS + t * P:n * TOKENS + (t + 1) * P],
                                            src[:, t, h * HEAD:(h + 1) * HEAD], identity[:, :])
                last.then_inc(qk_in_psum, 1)

            def scores(branch, h, head):
                pe.wait_ge(qk_copied, head + 1)
                q_t, k_t = qk_turned[:, 0, :], qk_turned[:, 1, :]
                for t, (a, b) in enumerate(((0, P), (P, 3 * P))):
                    last = pe.matmul(ps_scores[:, a:b], q_t[:, t * P:(t + 1) * P], k_t[:, 0:b - a],
                                     start=True, stop=branch == 1)
                    if branch == 0:
                        for part in (decay_high, decay_low):
                            minus = [part[:, u, h:h + 1].broadcast_to([P, P]) for u in range(TT)]
                            if t == 0:
                                last = pe.matmul(ps_scores[:, a:b], minus[0], up_to[:, 0:P],
                                                 start=False, stop=part is decay_low)
                            else:
                                pe.matmul(ps_scores[:, a:b], minus[0], up_to[:, :], start=False, stop=False)
                                last = pe.matmul(ps_scores[:, a + P:b], minus[1], up_to[:, 0:P],
                                                 start=False, stop=part is decay_low)
                last.then_inc(scores_in_psum, 1)

            def turn_probs(head):
                pe.wait_ge(probs_ready, head + 1)
                for n in range(3):
                    last = pe.transpose(ps_probs[:, n * P:(n + 1) * P], probs[:, n * P:(n + 1) * P], identity[:, :])
                last.then_inc(probs_in_psum, 1)

            def values(it, h, head):
                pair_v, use_v = pair_use(V_G, it)
                pe.wait_ge(evacuated[pair_v], use_v + 1)
                pe.wait_ge(probs_copied, head + 1)
                cols = slice(h * HEAD, (h + 1) * HEAD)
                pe.matmul(ps_o[:, 0:TOKENS], v_rows[:, 0, cols], probs_turned[:, 0:TOKENS], start=True, stop=False)
                pe.matmul(ps_o[:, P:TOKENS], v_rows[:, 1, cols], probs_turned[:, TOKENS:3 * P],
                          start=False, stop=True).then_inc(o_in_psum, 1)

            for branch in range(2):
                with pe.Fori(0, HALVES) as half:
                    it = half + HALVES * branch
                    for s in range(HALF_STEPS):
                        g, c = divmod(s, IN_STEPS)
                        if branch == 0 and s == IN_STEPS:
                            sum_decay(it)
                        for h in range(GROUP_HEADS):
                            head = it * GROUP_HEADS + h
                            at_step = s - HEAD_STEPS * h
                            if at_step == VALUES:
                                values(it, h, head)
                            if at_step == VALUES + 1:
                                pe.wait_ge(o_split, head + 1)
                            if at_step == TURN_QK:
                                turn_qk(it, h, head)
                            if at_step == SCORES:
                                scores(branch, h, head)
                        for h in range(GROUP_HEADS):
                            if s - HEAD_STEPS * h == TURN_P:
                                turn_probs(it * GROUP_HEADS + h)
                        pair, use = pair_use(g, it)
                        if c == 0 and g > Q_G:
                            pe.wait_ge(evacuated[pair], use)
                        multiply(Chunk(half, HALF_STEPS, HALVES * branch * HALF_STEPS + s), x_high, x_low,
                                 c * CHUNK_KT, pair, c == 0, c == IN_STEPS - 1)
                    pe.wait_ge(evacuated[1], pair_use(GATE0_G, it)[1] + 1)
                    pe.wait_ge(evacuated[0], pair_use(GATE1_G, it)[1] + 1)

            def merge_steps(n, first):
                for s in range(2 * O_STEPS):
                    branch, c = divmod(s, O_STEPS)
                    if s == 2 and not first:
                        pe.wait_ge(merged, n)
                        turn_block(merge_y, turn)
                    if s == 2 * O_STEPS - 1 and not first:
                        pe.wait_ge(block_split, n)
                    if c == 0:
                        pe.wait_ge(o_split, (branch + 1) * HEADS)
                        pe.wait_ge(evacuated[branch], n + U_MERGE[branch])
                    multiply(Chunk(n, 2 * O_STEPS, C_MERGE + s), o_high, o_low,
                             branch * HEADS + c * CHUNK_KT, branch, c == 0, c == O_STEPS - 1)

            merge_steps(0, True)
            with pe.Fori(1, OUT_GROUPS) as n:
                merge_steps(n, False)

            for n in range(OUT_GROUPS):
                pair, use = n % 2, U_OUT[n % 2] + n // 2
                for s in range(IN_STEPS):
                    if s == 2:
                        pe.wait_ge(block_split, B_OUT + n - 1)
                        if n == 0:
                            pe.wait_ge(merged, OUT_GROUPS)
                            turn_block(merge_y, turn)
                        else:
                            pe.wait_ge(evacuated[1 - pair], U_OUT[1 - pair] + (n - 1) // 2 + 1)
                            turn_block(rows[:, :, (n - 1) * COLS:n * COLS], turn)
                    if s == 0:
                        pe.wait_ge(block_split, B_OUT - 1)
                        pe.wait_ge(evacuated[pair], use)
                    if s == IN_STEPS - BLOCK_KT // CHUNK_KT:
                        pe.wait_ge(block_split, B_OUT)
                    multiply(Chunk(n, IN_STEPS, C_OUT + s), y_high, y_low, s * CHUNK_KT, pair,
                             s == 0, s == IN_STEPS - 1)

            def ff_steps(n, first):
                for s in range(2 * IN_STEPS):
                    pair, c = divmod(s, IN_STEPS)
                    if s == 2:
                        pe.wait_ge(block_split, n + B_FF - 1)
                        if first:
                            pe.wait_ge(evacuated[1], U_FF[1])
                            turn_block(rows[:, :, D - COLS:D], turn)
                        else:
                            pe.wait_ge(evacuated[1], n + U_FF[1])
                            turn_block(hidden_rows, turn)
                    if s == 0:
                        pe.wait_ge(block_split, B_FF - 1)
                    if c == 0:
                        pe.wait_ge(evacuated[pair], n + U_FF[pair])
                    if s == IN_STEPS - BLOCK_KT // CHUNK_KT and first:
                        pe.wait_ge(block_split, B_FF)
                    multiply(Chunk(n, 2 * IN_STEPS, C_FF + s), x2_high, x2_low, c * CHUNK_KT, pair,
                             c == 0, c == IN_STEPS - 1)

            ff_steps(0, True)
            with pe.Fori(1, FF_GROUPS) as n:
                ff_steps(n, False)
            pe.wait_ge(evacuated[1], U_DOWN[1])
            pe.wait_ge(block_split, B_FF + FF_GROUPS - 1)
            turn_block(hidden_rows, turn)

            with pe.Fori(0, OUT_GROUPS // 2) as i:
                for s in range(2 * FF_STEPS):
                    pair, c = divmod(s, FF_STEPS)
                    if c == 0:
                        pe.wait_ge(evacuated[pair], i + U_DOWN[pair])
                    if s == FF_STEPS - BLOCK_KT // CHUNK_KT:
                        pe.wait_ge(block_split, B_FF + FF_GROUPS)
                    multiply(Chunk(i, 2 * FF_STEPS, C_DOWN + s), h_high, h_low, c * CHUNK_KT, pair,
                             c == 0, c == FF_STEPS - 1)


_INS = ["x", "norm_mix", "w_in", "b_forget", "w_o_fox", "w_o_moba", "w_out", "norm_ffn", "w_gate_up", "w_down",
        "norm_final"]


def kernel(**inputs):
    import numpy as np
    import concourse.bacc as bacc
    from concourse.bass_utils import run_bass_kernel_spmd

    half = HEAD // 2
    inv_freq = np.float32(10000.0) ** (-np.arange(half, dtype=np.float32) / np.float32(half))
    angle = np.arange(TOKENS, dtype=np.float32)[:, None] * inv_freq[None, :].astype(np.float32)
    arrays = {name: np.ascontiguousarray(inputs[name]) for name in _INS}
    arrays["rope_cos"] = np.cos(angle).astype(np.float32)
    arrays["rope_sin"] = np.sin(angle).astype(np.float32)
    nc = bacc.Bacc("TRN2", target_bir_lowering=False, num_devices=1)
    args = [nc.dram_tensor(f"in_{name}", a.shape, F32, kind="ExternalInput").ap() for name, a in arrays.items()]
    args.append(nc.dram_tensor("out", (1, TOKENS, D), F32, kind="ExternalOutput").ap())
    build(nc, *args)
    r = run_bass_kernel_spmd(nc, [{f"in_{name}": a for name, a in arrays.items()}], core_ids=[0])
    return r.results[0]["out"]
```

```python
from contextlib import ExitStack

import concourse.bass as bass
from concourse import mybir

F32 = mybir.dt.float32
F32R = mybir.dt.float32r
ALU = mybir.AluOpType
ACT = mybir.ActivationFunctionType
AX = mybir.AxisListType

P = 128
TOKENS = 256
TT = TOKENS // P
D = 2048
HEAD = 128
HEADS = 8
WIDTH = HEADS * HEAD
D_FF = 5632
EPS = 1e-6
SCALE = float(HEAD) ** -0.5
MASKED = -1e30

COLS = 512
CHUNK_KT = 2
RING = 4
KT = D // P
FF_KT = D_FF // P
BLOCK_KT = COLS // P
IN_STEPS = KT // CHUNK_KT
O_STEPS = HEADS // CHUNK_KT
FF_STEPS = FF_KT // CHUNK_KT
GROUP_HEADS = COLS // HEAD
HALVES = HEADS // GROUP_HEADS
OUT_GROUPS = D // COLS
FF_GROUPS = D_FF // COLS

K_G, Q_G, V_G, GATE0_G, GATE1_G = range(5)
HALF_STEPS = 5 * IN_STEPS
TURN_QK, SCORES, TURN_P, VALUES, HEAD_STEPS = (18, 17, 17, 17), 19, 22, 26, 4
FORGET = 4

PASSES = 2 * HALVES
C_MERGE = PASSES * HALF_STEPS
C_OUT = C_MERGE + OUT_GROUPS * 2 * O_STEPS
C_FF = C_OUT + OUT_GROUPS * IN_STEPS
C_DOWN = C_FF + FF_GROUPS * 2 * IN_STEPS
CHUNKS = C_DOWN + OUT_GROUPS * FF_STEPS
PAIR_G = {K_G: (2, 1, 0), Q_G: (1, 2, 1), V_G: (0, 2, 1), GATE0_G: (1, 2, 2), GATE1_G: (0, 2, 2)}
PAIRS = (1, 0)
U_MERGE = 2 * PASSES + 1
U_OUT = U_MERGE + OUT_GROUPS
U_FF = U_OUT + OUT_GROUPS // 2
U_DOWN = U_FF + FF_GROUPS
WARM_UP = 18
ACT_RESULT, DVE_RESULT = (0, 3 * D // 8), ((3 * D // 8, 5 * D // 8), (5 * D // 8, D))
B_MERGE, B_OUT, B_FF = 0, OUT_GROUPS, 2 * OUT_GROUPS


class Chunk:

    def __init__(self, i, per, base):
        self.number = i * per + base
        self.slot = base % RING
        self.use = i * (per // RING) + base // RING
        self.early = isinstance(self.number, int) and self.number < RING


def columns(i, start=0):
    return bass.ds(i * COLS + start, COLS)


def build(nc, x, norm_mix, w_in, b_forget, w_o_fox, w_o_moba, w_out, norm_ffn, w_gate_up, w_down,
          norm_final, rope_cos, rope_sin, out):
    x_rows = x.rearrange("b (t p) n -> p (b t) n", p=P)
    out_rows = out.rearrange("b (t p) n -> p (b t) n", p=P)

    def chunked(w):
        return w.rearrange("l (c k p) n -> (l c) p k n", p=P, k=CHUNK_KT)

    w_in_c, w_fox_c, w_moba_c, w_out_c = chunked(w_in), chunked(w_o_fox), chunked(w_o_moba), chunked(w_out)
    w_ff_c, w_down_c = chunked(w_gate_up), chunked(w_down)
    F_COL = 3 * WIDTH * 2
    GATE_COL = F_COL + HEADS

    with ExitStack() as ctx:
        sem = lambda name: ctx.enter_context(nc.semaphore(name))
        psum = lambda name, shape: ctx.enter_context(nc.psum_tensor(name, shape, F32))

        base = (nc.sbuf_base + 63) // 64 * 64
        at = [base]

        def place(name, shape, dtype=F32, offset=None):
            size = 4
            for n in shape[1:]:
                size *= n
            size = (size + 31) // 32 * 32
            if offset is None:
                offset = at[0]
                at[0] += size
            t = nc.alloc_sbuf_tensor_at(name, shape, dtype, offset=offset)
            return t, offset + size

        weight_raw, _ = place("weight_raw", [P, RING, CHUNK_KT, COLS])
        weight_high, _ = place("weight_high", [P, RING, CHUNK_KT, COLS], F32R)
        weight_low, _ = place("weight_low", [P, RING, CHUNK_KT, COLS], F32R)
        rows, _ = place("rows", [P, TT, D])
        second = at[0]
        o_high, _ = place("o_high", [P, 2 * HEADS, TOKENS], F32R)
        o_low, _ = place("o_low", [P, 2 * HEADS, TOKENS], F32R)
        x2_high, end = place("x2_high", [P, KT, TOKENS], F32R, offset=second)
        x2_low, end = place("x2_low", [P, KT, TOKENS], F32R, offset=end)
        scaled_rows, end = place("scaled_rows", [P, TT, D], offset=second)
        first = at[0]
        x_high, _ = place("x_high", [P, KT, TOKENS], F32R)
        x_low, _ = place("x_low", [P, KT, TOKENS], F32R)
        y_high, end = place("y_high", [P, KT, TOKENS], F32R, offset=first)
        y_low, end = place("y_low", [P, KT, TOKENS], F32R, offset=end)
        gates, _ = place("gates", [P, 2, TT, D])
        k_rows, _ = place("k_rows", [P, TT, COLS])
        q_rows, _ = place("q_rows", [P, TT, COLS])
        v_high, _ = place("v_high", [P, TT, COLS], F32R)
        v_low, _ = place("v_low", [P, TT, COLS], F32R)
        rope_a, _ = place("rope_a", [P, TT, COLS])
        rope_b, _ = place("rope_b", [P, TT, COLS])
        qk_high, _ = place("qk_high", [P, 2, TOKENS], F32R)
        qk_low, _ = place("qk_low", [P, 2, TOKENS], F32R)
        logits, _ = place("logits", [P, 3 * P])
        probs, _ = place("probs", [P, 3 * P])
        p_high, _ = place("p_high", [P, 3 * P], F32R)
        p_low, _ = place("p_low", [P, 3 * P], F32R)
        h_high, end = place("h_high", [P, FF_KT, TOKENS], F32R, offset=first)
        h_low, end = place("h_low", [P, FF_KT, TOKENS], F32R, offset=end)
        merge_a, end = place("merge_a", [P, TT, COLS], offset=end)
        merge_b, end = place("merge_b", [P, TT, COLS], offset=end)
        at[0] = max(at[0], end)
        identity, _ = place("identity", [P, P])
        causal, _ = place("causal", [P, 3 * P])
        up_to, _ = place("up_to", [P, 3 * P], F32R)
        gain_rows, _ = place("gain_rows", [KT, 2, P])
        gains, _ = place("gains", [P, 2, KT])
        w_forget, _ = place("w_forget", [P, KT, HEADS])
        w_forget_high, _ = place("w_forget_high", [P, KT, HEADS], F32R)
        w_forget_low, _ = place("w_forget_low", [P, KT, HEADS], F32R)
        bias_forget, _ = place("bias_forget", [P, HEADS])
        rope, _ = place("rope", [P, 2, TT, HEAD // 2])
        rope_kq, _ = place("rope_kq", [P, 2, 2, TT, HEAD // 2])
        forget_turned, _ = place("forget_turned", [HEADS, TOKENS])
        forget_rows, _ = place("forget_rows", [P, TT, HEADS])
        forget, _ = place("forget", [P, 5, TT, GROUP_HEADS])
        decay_rows, _ = place("decay_rows", [P, TT, GROUP_HEADS])
        decay_high, _ = place("decay_high", [P, TT, GROUP_HEADS], F32R)
        decay_low, _ = place("decay_low", [P, TT, GROUP_HEADS], F32R)
        decay_sum, _ = place("decay_sum", [P, TT, GROUP_HEADS])
        squares, _ = place("squares", [P, 4, TT, OUT_GROUPS])
        mean_square, _ = place("mean_square", [P, 4, TT])
        norm_tmp, _ = place("norm_tmp", [P, 4, 6, TT])
        rstd, _ = place("rstd", [P, 4, TT])
        eps, _ = place("eps", [P, 1])
        rstd_q, _ = place("rstd_q", [P, TT])
        row_max_neg, _ = place("row_max_neg", [P, TT])
        row_sum, _ = place("row_sum", [P, TT])
        row_sum_inv, _ = place("row_sum_inv", [P, TT])
        ones, _ = place("ones", [P, 3 * P])
        merge = (merge_a, merge_b)
        merge_y, silu, hidden_rows = k_rows, merge_a, merge_b
        final_gain, _ = place("final_gain", [P, D], offset=second + 4 * TT * D)

        acc = [psum(f"acc{n}", [P, TT, COLS]) for n in range(2)]
        turn2 = psum("turn2", [P, 2, COLS])
        acc.append(turn2)
        turn = psum("turn", [P, 2, COLS])
        ps_qk, ps_scores, ps_probs, ps_o = turn[:, 0, :], turn[:, 1, :], turn2[:, 0, :], turn2[:, 1, :]
        ps_forget_turned = acc[0][0:HEADS, 0, 0:TOKENS]
        ps_forget = acc[0][:, 1, 0:TT * HEADS].rearrange("p (t h) -> p t h", t=TT)
        ps_gain = acc[1][:, 1, 0:2 * KT].rearrange("p (g k) -> p g k", g=2)
        turned_x = (turn, turn2, acc[1], turn)

        small_landed, wf_landed, gain_landed, fin_landed = map(
            sem, ("small_landed", "wf_landed", "gain_landed", "fin_landed"))
        x_landed = [sem(f"x_landed{n}") for n in range(OUT_GROUPS)]
        stored = sem("stored")
        raw_landed = [sem(f"raw_landed{n}") for n in range(RING)]
        raw_free = sem("raw_free")
        high_ready = sem("high_ready")
        chunk_used = sem("chunk_used")
        evacuated = [sem(f"evacuated{n}") for n in range(3)]
        zeroed, consts = sem("zeroed"), sem("consts")
        gains_turned = sem("gains_turned")
        x_turned, x_rounded, x_split = sem("x_turned"), sem("x_rounded"), sem("x_split")
        wf_rounded, wf_split = sem("wf_rounded"), sem("wf_split")
        forget_multiplied, forget_taken, forget_logits = map(
            sem, ("forget_multiplied", "forget_taken", "forget_logits"))
        eps_ready = sem("eps_ready")
        squares_ready = sem("squares_ready")
        norm_vec, norm_act = sem("norm_vec"), sem("norm_act")
        squares_summed, rstd_ready, rstd_q_ready = sem("squares_summed"), sem("rstd_ready"), sem("rstd_q_ready")
        forget_vec, forget_act = sem("forget_vec"), sem("forget_act")
        decay_rounded, decay_split = sem("decay_rounded"), sem("decay_split")
        decay_summed, decay_ready = sem("decay_summed"), sem("decay_ready")
        rope_vec = sem("rope_vec")
        qk_in_psum, qk_rounded, qk_split = sem("qk_in_psum"), sem("qk_rounded"), sem("qk_split")
        v_rounded = sem("v_rounded")
        scores_in_psum, scores_masked = sem("scores_in_psum"), sem("scores_masked")
        row_max_ready, exp_done = sem("row_max_ready"), sem("exp_done")
        row_sum_inverted, probs_ready = sem("row_sum_inverted"), sem("probs_ready")
        p_in_psum, p_rounded, p_split = sem("p_in_psum"), sem("p_rounded"), sem("p_split")
        o_in_psum, o_rounded, o_split = sem("o_in_psum"), sem("o_rounded"), sem("o_split")
        gate_ready = sem("gate_ready")
        merged = sem("merged")
        block_turned, block_rounded, block_split = sem("block_turned"), sem("block_rounded"), sem("block_split")
        tile_done, rows_added, final_scaled = sem("tile_done"), sem("rows_added"), sem("final_scaled")
        result_act, result_dve = sem("result_act"), sem("result_dve")

        def split_count(chunk):
            return chunk.number + RING + 1

        def pair_use(g, it):
            pair, per, n = PAIR_G[g]
            return pair, it * per + n

        block = ctx.enter_context(nc.Block())

        @block.sync
        def _(sp):
            for b in range(OUT_GROUPS):
                piece = slice(b * COLS, (b + 1) * COLS)
                sp.dma_start(rows[:, :, piece], x_rows[:, :, piece]).then_inc(x_landed[b], 16)
            sp.sem_inc(raw_free, RING)

            def load(chunk, source):
                sp.wait_ge(raw_free, chunk.number + 1)
                sp.dma_start(weight_raw[:, chunk.slot, :, :], source).then_inc(raw_landed[chunk.slot], 16)

            for branch in range(2):
                with sp.Fori(1, HALVES + 1) as half_1:
                    at0 = 3 * WIDTH * branch
                    gate = GATE_COL + D * branch
                    first_col = [half_1 * COLS + (at0 + WIDTH - COLS), half_1 * COLS + (at0 - COLS),
                                 half_1 * COLS + (at0 + 2 * WIDTH - COLS),
                                 half_1 * (2 * COLS) + (gate - 2 * COLS), half_1 * (2 * COLS) + (gate - COLS)]
                    for g in range(5):
                        for c in range(IN_STEPS):
                            load(Chunk(half_1 - 1, HALF_STEPS, HALVES * branch * HALF_STEPS + g * IN_STEPS + c),
                                 w_in_c[c][:, :, bass.ds(first_col[g], COLS)])
            with sp.Fori(1, OUT_GROUPS + 1) as n_1:
                for c in range(2 * O_STEPS):
                    w = w_fox_c if c < O_STEPS else w_moba_c
                    load(Chunk(n_1 - 1, 2 * O_STEPS, C_MERGE + c), w[c % O_STEPS][:, :, columns(n_1, -COLS)])
            with sp.Fori(1, OUT_GROUPS + 1) as n_1:
                for c in range(IN_STEPS):
                    load(Chunk(n_1 - 1, IN_STEPS, C_OUT + c), w_out_c[c][:, :, columns(n_1, -COLS)])
            with sp.Fori(1, FF_GROUPS + 1) as n_1:
                for c in range(2 * IN_STEPS):
                    load(Chunk(n_1 - 1, 2 * IN_STEPS, C_FF + c),
                         w_ff_c[c % IN_STEPS][:, :, columns(n_1, D_FF * (c // IN_STEPS) - COLS)])
            with sp.Fori(1, OUT_GROUPS // 2 + 1) as i_1:
                for c in range(2 * FF_STEPS):
                    load(Chunk(i_1 - 1, 2 * FF_STEPS, C_DOWN + c),
                         w_down_c[c % FF_STEPS][:, :, bass.ds(i_1 * (2 * COLS) + COLS * (c // FF_STEPS - 2), COLS)])
            for t in range(TT):
                for ready, count, (a, b) in ((result_dve, 2 * t + 1, DVE_RESULT[0]), (result_act, t + 1, ACT_RESULT),
                                             (result_dve, 2 * t + 2, DVE_RESULT[1])):
                    sp.wait_ge(ready, count)
                    sp.dma_start(out_rows[:, t, a:b], scaled_rows[:, t, a:b]).then_inc(stored, 16)
            sp.wait_ge(stored, 16 * 3 * TT)

        @block.gpsimd
        def _(pool):
            pool.memset(eps[:, :], EPS).then_inc(eps_ready, 1)
            pool.memset(identity[:, :], 0.0).then_inc(zeroed, 1)
            pool.memset(causal[:, :], 0.0).then_inc(zeroed, 1)
            pool.memset(ones[:, :], 1.0).then_inc(zeroed, 1)
            pool.wait_ge(zeroed, 3)
            pool.affine_select(out=identity[:, :], in_=identity[:, :], compare_op=ALU.not_equal, fill=1.0,
                               base=0, pattern=[[-1, P]], channel_multiplier=1).then_inc(consts, 1)
            for n in (0, 2):
                own = causal[:, n * P:(n + 1) * P]
                pool.affine_select(out=own, in_=own, compare_op=ALU.is_ge, fill=MASKED,
                                   base=0, pattern=[[-1, P]], channel_multiplier=1).then_inc(consts, 1)
            for n in range(2):
                own = ones[:, n * P:(n + 1) * P]
                pool.affine_select(out=own, in_=own, compare_op=ALU.is_ge, fill=0.0,
                                   base=0, pattern=[[1, P]], channel_multiplier=-1).then_inc(consts, 1)
            pool.wait_ge(consts, 5)
            pool.tensor_copy(up_to[:, :], ones[:, :]).then_inc(consts, 1)
            pool.dma_start(bias_forget[:, :], b_forget.broadcast_to([P, HEADS])).then_inc(small_landed, 16)
            for n, table in enumerate((rope_cos, rope_sin)):
                pool.dma_start(rope[:, n, :, :], table.rearrange("(t p) d -> p t d", p=P))\
                   .then_inc(small_landed, 16)

        @block.scalar
        def _(act):
            for n, g in enumerate((norm_mix, norm_ffn)):
                act.dma_start(gain_rows[:, n, :], g.rearrange("l (k p) -> (l k) p", p=P))\
                   .then_inc(gain_landed, 16)
            act.dma_start(w_forget[:, :, :], w_in.rearrange("l (k p) n -> p (l k) n", p=P)[:, :, F_COL:GATE_COL])\
               .then_inc(wf_landed, 16)

            def round_chunk(chunk):
                act.wait_ge(raw_landed[chunk.slot], chunk.use * 16 + 16)
                if not chunk.early:
                    act.wait_ge(chunk_used, chunk.number - RING + 1)
                act.activation(weight_high[:, chunk.slot, :, :], weight_raw[:, chunk.slot, :, :], ACT.Copy)\
                   .then_inc(high_ready, 1)

            def round_block(dst, kt, scales, number):
                act.wait_ge(block_turned, number + 1)
                if scales is None:
                    act.activation(dst[:, bass.ds(kt, BLOCK_KT), :],
                                   turn[:, :, :].rearrange("p a (j n) -> p (a j) n", n=TOKENS), ACT.Copy)\
                       .then_inc(block_rounded, 1)
                    return
                for j in range(BLOCK_KT):
                    last = act.activation(dst[:, kt + j, :], turn[:, j // 2, (j % 2) * TOKENS:(j % 2 + 1) * TOKENS],
                                          ACT.Copy, scale=scales[:, kt + j:kt + j + 1])
                last.then_inc(block_rounded, 1)

            def root(n, t=slice(0, TT)):
                act.wait_ge(squares_summed, n + 1)
                act.activation(norm_tmp[:, n, 0, t], norm_tmp[:, n, 5, t], ACT.Sqrt, scale=1.0 / D,
                               bias=eps[:, 0:1]).then_inc(norm_act, 1)

            def load_root_table():
                act.activation(norm_tmp[:, 0, 4, 0:1], eps[:, 0:1], ACT.Sqrt)

            def square_piece(b):
                act.wait_ge(x_landed[b], 16)
                for t in range(TT):
                    piece = slice(b * COLS, (b + 1) * COLS)
                    last = act.activation(gates[:, 0, t, piece], rows[:, t, piece], ACT.Square,
                                          accum_out=squares[:, 0, t, b:b + 1])
                if b == OUT_GROUPS - 1:
                    last.then_inc(squares_ready, 1)

            act.wait_ge(eps_ready, 1)
            load_root_table()
            act.wait_ge(wf_landed, 16)
            act.activation(w_forget_high[:, :, :], w_forget[:, :, :], ACT.Copy).then_inc(wf_rounded, 1)
            act.wait_ge(evacuated[1], 1)
            for b in range(KT // BLOCK_KT):
                act.wait_ge(x_turned, b + 1)
                for j in range(BLOCK_KT):
                    kt = b * BLOCK_KT + j
                    act.activation(x_high[:, kt, :], turned_x[b][:, j // 2, (j % 2) * TOKENS:(j % 2 + 1) * TOKENS],
                                   ACT.Copy, scale=gains[:, 0, kt:kt + 1]).then_inc(x_rounded, 1)
            round_chunk(Chunk(0, RING, 0))
            round_chunk(Chunk(0, RING, 1))
            square_piece(0)
            act.wait_ge(forget_multiplied, 1)
            act.activation(forget_turned[:, :], ps_forget_turned, ACT.Copy).then_inc(forget_taken, 1)
            round_chunk(Chunk(0, RING, 2))
            round_chunk(Chunk(0, RING, 3))
            for b in range(1, OUT_GROUPS):
                square_piece(b)
            root(0)
            act.wait_ge(rstd_ready, 1)

            def take_out(dst, g, it, half, branch, scales):
                pair, use = pair_use(g, it)
                act.wait_ge(chunk_used, Chunk(half, HALF_STEPS, HALVES * branch * HALF_STEPS
                                              + (g + 1) * IN_STEPS - 1).number + 1)
                for t in range(TT):
                    last = act.activation(dst[:, t, :], acc[pair][:, t, :], ACT.Copy, scale=scales[:, t:t + 1])
                last.then_inc(v_rounded if g == V_G else evacuated[pair], 1)

            def take_out_gate(g, it, half, branch):
                pair, _ = pair_use(g, it)
                act.wait_ge(chunk_used, Chunk(half, HALF_STEPS, HALVES * branch * HALF_STEPS
                                              + (g + 1) * IN_STEPS - 1).number + 1)
                for t in range(TT):
                    last = act.activation(gates[:, branch, t, bass.ds(half * 2 * COLS + COLS * (g - GATE0_G), COLS)],
                                          acc[pair][:, t, :], ACT.Copy, scale=rstd[:, 0, t:t + 1])
                last.then_inc(evacuated[pair], 1)

            for branch in range(2):
                with act.Fori(0, HALVES) as half:
                    it = half + HALVES * branch
                    for s in range(HALF_STEPS):
                        if branch == 0 and s == FORGET:
                            act.wait_ge(forget_vec, it * 4 + 3)
                            act.activation(forget[:, 3, :, :], forget[:, 1, :, :], ACT.Exp, scale=-1.0)\
                               .then_inc(forget_act, 1)
                            act.wait_ge(forget_act, it * 2 + 1)
                            act.activation(forget[:, 4, :, :], forget[:, 3, :, :], ACT.Ln, bias=1.0)\
                               .then_inc(forget_act, 1)
                        if branch == 0 and s == IN_STEPS - 1:
                            take_out(k_rows, K_G, it, half, branch, rstd[:, 0, :])
                        if branch == 0 and s == 2 * IN_STEPS - 1:
                            take_out(q_rows, Q_G, it, half, branch, rstd_q)
                        for h in range(GROUP_HEADS):
                            head = it * GROUP_HEADS + h
                            at_step = s - HEAD_STEPS * h
                            if at_step == VALUES:
                                act.wait_ge(o_in_psum, head + 1)
                                act.activation(o_high[:, bass.ds(head, 1), :],
                                               ps_o[:, 0:TOKENS].unsqueeze(1), ACT.Copy).then_inc(o_rounded, 1)
                            if at_step == TURN_QK[h]:
                                act.wait_ge(qk_in_psum, head + 1)
                                act.activation(qk_high[:, :, :].rearrange("p a n -> p (a n)"), ps_qk, ACT.Copy)\
                                   .then_inc(qk_rounded, 1)
                            if at_step == SCORES:
                                act.wait_ge(row_max_ready, head + 1)
                                act.activation(probs[:, 0:P], logits[:, 0:P], ACT.Exp,
                                               bias=row_max_neg[:, 0:1], accum_out=row_sum[:, 0:1])
                                act.activation(probs[:, P:3 * P], logits[:, P:3 * P], ACT.Exp,
                                               bias=row_max_neg[:, 1:2], accum_out=row_sum[:, 1:2])\
                                   .then_inc(exp_done, 1)
                            if at_step == TURN_P:
                                act.wait_ge(p_in_psum, head + 1)
                                act.activation(p_high[:, :], ps_probs[:, 0:3 * P], ACT.Copy).then_inc(p_rounded, 1)
                        if s == 3 * IN_STEPS - 1:
                            take_out(v_high, V_G, it, half, branch, rstd[:, 0, :])
                        if s == 4 * IN_STEPS - 1:
                            take_out_gate(GATE0_G, it, half, branch)
                        if s == HALF_STEPS - 1:
                            take_out_gate(GATE1_G, it, half, branch)
                        round_chunk(Chunk(half, HALF_STEPS, HALVES * branch * HALF_STEPS + s + RING))

            def merge_steps(n, first):
                for s in range(2 * O_STEPS):
                    if s % O_STEPS == 0:
                        branch = s // O_STEPS
                        if not first and s == 0:
                            act.wait_ge(merged, n)
                        act.activation(merge[branch][:, :, :], gates[:, branch, :, columns(n)], ACT.Sigmoid)\
                           .then_inc(gate_ready, 1)
                    if s == 2 and not first:
                        round_block(y_high, (n - 1) * BLOCK_KT, None, n + B_MERGE - 1)
                    round_chunk(Chunk(n, 2 * O_STEPS, C_MERGE + s + RING))

            merge_steps(0, True)
            with act.Fori(1, OUT_GROUPS) as n:
                merge_steps(n, False)

            def sum_squares(sums, t, n):
                return act.activation(merge_a[:, t, :], rows[:, t, n * COLS:(n + 1) * COLS], ACT.Square,
                                      accum_out=sums[:, t, n:n + 1])

            for n in range(OUT_GROUPS):
                for s in range(IN_STEPS):
                    if s == 2:
                        if n == 0:
                            round_block(y_high, (OUT_GROUPS - 1) * BLOCK_KT, None, B_OUT - 1)
                        else:
                            round_block(x2_high, (n - 1) * BLOCK_KT, gains[:, 1, :], B_OUT + n - 1)
                    if s == IN_STEPS - 1:
                        act.wait_ge(evacuated[PAIRS[n % 2]], U_OUT + n // 2 + 1)
                        for t in range(TT):
                            last = sum_squares(squares[:, 1, :, :], t, n)
                        if n == OUT_GROUPS - 1:
                            last.then_inc(squares_ready, 1)
                    round_chunk(Chunk(n, IN_STEPS, C_OUT + s + RING))

            def ff_steps(n, first):
                for s in range(2 * IN_STEPS):
                    if s == 0 and first:
                        root(1)
                    if s == 2:
                        if first:
                            round_block(x2_high, (OUT_GROUPS - 1) * BLOCK_KT, gains[:, 1, :], B_FF - 1)
                        else:
                            round_block(h_high, (n - 1) * BLOCK_KT, None, n + B_FF - 1)
                    if s == IN_STEPS - 1:
                        if first:
                            act.wait_ge(rstd_ready, 2)
                        act.wait_ge(chunk_used, Chunk(n, 2 * IN_STEPS, C_FF + s).number + 1)
                        for t in range(TT):
                            last = act.activation(silu[:, t, :], acc[PAIRS[0]][:, t, :], ACT.Silu,
                                                  scale=rstd[:, 1, t:t + 1])
                        last.then_inc(evacuated[PAIRS[0]], 1)
                    round_chunk(Chunk(n, 2 * IN_STEPS, C_FF + s + RING))

            ff_steps(0, True)
            with act.Fori(1, FF_GROUPS) as n:
                ff_steps(n, False)

            act.wait_ge(chunk_used, C_DOWN)
            act.dma_start(final_gain[:, :], norm_final.rearrange("(a n) -> a n", a=1).broadcast_to([P, D]))\
               .then_inc(fin_landed, 16)
            load_root_table()
            for n in range(OUT_GROUPS):
                for s in range(FF_STEPS):
                    if n == 0 and s == 2:
                        round_block(h_high, (FF_GROUPS - 1) * BLOCK_KT, None, B_FF + FF_GROUPS - 1)
                    if s == FF_STEPS - 1 and n < OUT_GROUPS - 1:
                        act.wait_ge(evacuated[PAIRS[n % 2]], U_DOWN + n // 2 + 1)
                        for t in range(TT):
                            sum_squares(squares[:, 2 + t, :, :], t, n)
                    if C_DOWN + n * FF_STEPS + s + RING < CHUNKS:
                        round_chunk(Chunk(0, RING, C_DOWN + n * FF_STEPS + s + RING))
            for t in range(TT):
                act.wait_ge(rows_added, t + 1)
                sum_squares(squares[:, 2 + t, :, :], t, OUT_GROUPS - 1).then_inc(squares_ready, 1)
                root(2 + t, slice(t, t + 1))
                act.wait_ge(rstd_ready, 3 + t)
                act.wait_ge(final_scaled, OUT_GROUPS + t)
                piece = scaled_rows[:, t, slice(*ACT_RESULT)]
                act.activation(piece, piece, ACT.Copy, scale=rstd[:, 2 + t, t:t + 1]).then_inc(result_act, 1)

        @block.vector
        def _(dve):
            def rest_of_chunk(chunk):
                dve.wait_ge(high_ready, chunk.number + 1)
                dve.tensor_tensor(weight_low[:, chunk.slot, :, :], weight_raw[:, chunk.slot, :, :],
                                  weight_high[:, chunk.slot, :, :].bitcast(F32), ALU.subtract)\
                   .then_inc(raw_free, 1)

            def rest_of_block(high, low, kt, scales, number):
                dve.wait_ge(block_rounded, number + 1)
                if scales is None:
                    dve.tensor_tensor(low[:, bass.ds(kt, BLOCK_KT), :],
                                      turn[:, :, :].rearrange("p a (j n) -> p (a j) n", n=TOKENS),
                                      high[:, bass.ds(kt, BLOCK_KT), :].bitcast(F32), ALU.subtract)\
                       .then_inc(block_split, 1)
                    return
                for j in range(BLOCK_KT):
                    last = dve.scalar_tensor_tensor(
                        out=low[:, kt + j, :], in0=turn[:, j // 2, (j % 2) * TOKENS:(j % 2 + 1) * TOKENS],
                        scalar=scales[:, kt + j:kt + j + 1], in1=high[:, kt + j, :].bitcast(F32),
                        op0=ALU.mult, op1=ALU.subtract)
                last.then_inc(block_split, 1)

            def root(n, t=slice(0, TT)):
                v, root_v, total = mean_square[:, n, t], norm_tmp[:, n, 0, t], norm_tmp[:, n, 5, t]
                y0, t1, t2 = (norm_tmp[:, n, 1 + k, t] for k in range(3))
                dve.wait_ge(squares_ready, n + 1)
                dve.tensor_reduce(total, squares[:, n, t, :], AX.X, ALU.add)\
                   .then_inc(squares_summed, 1)
                dve.wait_ge(squares_summed, n + 1)
                dve.tensor_scalar(v, total, 1.0 / D, EPS, ALU.mult, ALU.add).then_inc(norm_vec, 1)
                dve.wait_ge(norm_act, n + 1)
                dve.reciprocal(y0, root_v).then_inc(norm_vec, 1)
                dve.wait_ge(norm_vec, 4 * n + 2)
                dve.tensor_tensor(t1, y0, y0, ALU.mult).then_inc(norm_vec, 1)
                dve.wait_ge(norm_vec, 4 * n + 3)
                dve.scalar_tensor_tensor(out=t2, in0=v, scalar=-0.5, in1=t1, op0=ALU.mult, op1=ALU.mult)\
                   .then_inc(norm_vec, 1)
                dve.wait_ge(norm_vec, 4 * n + 4)
                dve.scalar_tensor_tensor(out=rstd[:, n, t], in0=t2, scalar=1.5, in1=y0, op0=ALU.add, op1=ALU.mult)\
                   .then_inc(rstd_ready, 1)
                dve.wait_ge(rstd_ready, n + 1)

            dve.wait_ge(gains_turned, 1)
            dve.tensor_copy(gains[:, :, :], ps_gain).then_inc(evacuated[1], 1)
            dve.wait_ge(evacuated[1], 1)
            dve.wait_ge(wf_rounded, 1)
            dve.tensor_tensor(w_forget_low[:, :, :], w_forget[:, :, :], w_forget_high[:, :, :].bitcast(F32),
                              ALU.subtract).then_inc(wf_split, 1)
            for kt in range(KT):
                b, j = divmod(kt, BLOCK_KT)
                if kt % 2 == 0:
                    dve.wait_ge(x_rounded, kt + 2)
                dve.scalar_tensor_tensor(
                    out=x_low[:, kt, :], in0=turned_x[b][:, j // 2, (j % 2) * TOKENS:(j % 2 + 1) * TOKENS],
                    scalar=gains[:, 0, kt:kt + 1], in1=x_high[:, kt, :].bitcast(F32),
                    op0=ALU.mult, op1=ALU.subtract).then_inc(x_split, 1)
            for c in range(RING):
                rest_of_chunk(Chunk(0, RING, c))
            dve.wait_ge(forget_logits, 1)
            dve.tensor_copy(forget_rows[:, :, :], ps_forget).then_inc(evacuated[0], 1)
            root(0)
            dve.tensor_scalar(rstd_q[:, :], rstd[:, 0, :], SCALE, None, ALU.mult).then_inc(rstd_q_ready, 1)
            dve.wait_ge(rstd_q_ready, 1)
            dve.wait_ge(evacuated[0], 1)
            dve.wait_ge(small_landed, 48)

            def rope_tables():
                for kq in range(2):
                    for t in range(TT):
                        for cs in range(2):
                            scale = rstd[:, 0, t:t + 1] if kq == 0 else rstd_q[:, t:t + 1]
                            dve.tensor_scalar(rope_kq[:, kq, cs, t, :], rope[:, cs, t, :], scale, None, ALU.mult)\
                               .then_inc(rope_vec, 1)
                dve.wait_ge(rope_vec, 8)

            def forget_gates(it):
                heads = bass.ds(it * GROUP_HEADS, GROUP_HEADS)
                for t in range(TT):
                    last = dve.scalar_tensor_tensor(out=forget[:, 0, t, :], in0=forget_rows[:, t, heads],
                                                    scalar=rstd[:, 0, t:t + 1], in1=bias_forget[:, heads],
                                                    op0=ALU.mult, op1=ALU.add)
                last.then_inc(forget_vec, 1)
                dve.wait_ge(forget_vec, it * 4 + 1)
                dve.tensor_scalar(forget[:, 2, :, :], forget[:, 0, :, :], -1.0, None, ALU.mult).then_inc(forget_vec, 1)
                dve.wait_ge(forget_vec, it * 4 + 2)
                dve.tensor_tensor(forget[:, 1, :, :], forget[:, 0, :, :], forget[:, 2, :, :], ALU.max)\
                   .then_inc(forget_vec, 1)

            def split_decay(it):
                dve.wait_ge(forget_act, it * 2 + 2)
                dve.scalar_tensor_tensor(out=decay_rows[:, :, :].rearrange("p t h -> p (t h)"),
                                         in0=forget[:, 2, :, :].rearrange("p t h -> p (t h)"), scalar=0.0,
                                         in1=forget[:, 4, :, :].rearrange("p t h -> p (t h)"),
                                         op0=ALU.max, op1=ALU.add).then_inc(forget_vec, 1)
                dve.wait_ge(forget_vec, it * 4 + 4)
                dve.tensor_copy(decay_high[:, :, :], decay_rows[:, :, :]).then_inc(decay_rounded, 1)
                dve.wait_ge(decay_rounded, it + 1)
                dve.tensor_tensor(decay_low[:, :, :], decay_rows[:, :, :], decay_high[:, :, :].bitcast(F32),
                                  ALU.subtract).then_inc(decay_split, 1)

            rope_tables()

            def rotate(dst, g, it, half, branch, kq, turn_no):
                pair, use = pair_use(g, it)
                dve.wait_ge(chunk_used, Chunk(half, HALF_STEPS, HALVES * branch * HALF_STEPS
                                              + (g + 1) * IN_STEPS - 1).number + 1)
                src = acc[pair][:, :, :].rearrange("p t (e d) -> p t e d", d=HEAD // 2)
                for cs, tmp in ((0, rope_a), (1, rope_b)):
                    table = rope_kq[:, kq, cs, :, :].unsqueeze(2).broadcast_to([P, TT, COLS // (HEAD // 2), HEAD // 2])
                    dve.tensor_tensor(tmp[:, :, :].rearrange("p t (e d) -> p t e d", d=HEAD // 2), src, table,
                                      ALU.mult).then_inc(rope_vec, 1)
                done = half * 6 + 8 + 3 * turn_no
                dve.wait_ge(rope_vec, done + 2)
                halves = lambda a: a[:, :, :].rearrange("p t (h e d) -> p (t h) e d", e=2, d=HEAD // 2)
                o, a, b = halves(dst), halves(rope_a), halves(rope_b)
                dve.tensor_tensor(o[:, :, 0, :], a[:, :, 0, :], b[:, :, 1, :], ALU.subtract).then_inc(rope_vec, 1)
                dve.tensor_tensor(o[:, :, 1, :], a[:, :, 1, :], b[:, :, 0, :], ALU.add).then_inc(evacuated[pair], 1)

            for branch in range(2):
                with dve.Fori(0, HALVES) as half:
                    it = half + HALVES * branch
                    for s in range(HALF_STEPS):
                        if branch == 0 and s == FORGET:
                            forget_gates(it)
                        if branch == 0 and s == FORGET + 2:
                            split_decay(it)
                        if branch == 0 and s == IN_STEPS + 1:
                            dve.wait_ge(decay_summed, it + 1)
                            dve.tensor_scalar(decay_sum[:, :, :], ps_probs[:, 0:TT * GROUP_HEADS]
                                              .rearrange("p (t h) -> p t h", t=TT), -1.0, None, ALU.mult)\
                               .then_inc(decay_ready, 1)
                            dve.wait_ge(decay_ready, it + 1)
                        if branch == 1 and s == IN_STEPS - 1:
                            rotate(k_rows, K_G, it, half, branch, 0, 0)
                        if branch == 1 and s == 2 * IN_STEPS - 1:
                            rotate(q_rows, Q_G, it, half, branch, 1, 1)
                        for h in range(GROUP_HEADS):
                            head = it * GROUP_HEADS + h
                            at_step = s - HEAD_STEPS * h
                            if at_step == VALUES:
                                dve.wait_ge(o_rounded, head + 1)
                                dve.tensor_tensor(o_low[:, bass.ds(head, 1), :], ps_o[:, 0:TOKENS].unsqueeze(1),
                                                  o_high[:, bass.ds(head, 1), :].bitcast(F32), ALU.subtract)\
                                   .then_inc(o_split, 1)
                            if at_step == TURN_QK[h]:
                                dve.wait_ge(qk_rounded, head + 1)
                                dve.tensor_tensor(qk_low[:, :, :].rearrange("p a n -> p (a n)"), ps_qk,
                                                  qk_high[:, :, :].rearrange("p a n -> p (a n)").bitcast(F32),
                                                  ALU.subtract).then_inc(qk_split, 1)
                            if at_step == TURN_P:
                                dve.wait_ge(p_rounded, head + 1)
                                dve.tensor_tensor(p_low[:, :], ps_probs[:, 0:3 * P], p_high[:, :].bitcast(F32),
                                                  ALU.subtract).then_inc(p_split, 1)
                            if at_step == SCORES:
                                dve.wait_ge(scores_in_psum, head + 1)
                                if branch == 0:
                                    for t, (a, b) in enumerate(((0, P), (P, 3 * P))):
                                        last = dve.scalar_tensor_tensor(
                                            out=logits[:, a:b], in0=ps_scores[:, a:b], scalar=decay_sum[:, t, h:h + 1],
                                            in1=causal[:, a:b], op0=ALU.add, op1=ALU.add)
                                    last.then_inc(scores_masked, 1)
                                else:
                                    dve.tensor_tensor(logits[:, :], ps_scores[:, 0:3 * P], causal[:, :], ALU.add)\
                                       .then_inc(scores_masked, 1)
                                dve.wait_ge(scores_masked, head + 1)
                                dve.tensor_reduce(row_max_neg[:, 0:1], logits[:, 0:P], AX.X, ALU.max, negate=True)
                                dve.tensor_reduce(row_max_neg[:, 1:2], logits[:, P:3 * P], AX.X, ALU.max, negate=True)\
                                   .then_inc(row_max_ready, 1)
                            if at_step == SCORES + 1:
                                dve.wait_ge(exp_done, head + 1)
                                dve.reciprocal(row_sum_inv[:, :], row_sum[:, :]).then_inc(row_sum_inverted, 1)
                                dve.wait_ge(row_sum_inverted, head + 1)
                                dve.tensor_scalar(probs[:, 0:P], probs[:, 0:P], row_sum_inv[:, 0:1], None, ALU.mult)
                                dve.tensor_scalar(probs[:, P:3 * P], probs[:, P:3 * P], row_sum_inv[:, 1:2], None,
                                                  ALU.mult).then_inc(probs_ready, 1)
                        if s == 3 * IN_STEPS - 1:
                            pair, _ = pair_use(V_G, it)
                            dve.wait_ge(v_rounded, it + 1)
                            for t in range(TT):
                                last = dve.scalar_tensor_tensor(
                                    out=v_low[:, t, :], in0=acc[pair][:, t, :], scalar=rstd[:, 0, t:t + 1],
                                    in1=v_high[:, t, :].bitcast(F32), op0=ALU.mult, op1=ALU.subtract)
                            last.then_inc(evacuated[pair], 1)
                        rest_of_chunk(Chunk(half, HALF_STEPS, HALVES * branch * HALF_STEPS + s + RING))

            def merge_steps(n, first):
                for s in range(2 * O_STEPS):
                    if s == 2 and not first:
                        rest_of_block(y_high, y_low, (n - 1) * BLOCK_KT, None, n + B_MERGE - 1)
                    for branch, dst in enumerate(merge):
                        if s == (branch + 1) * O_STEPS - 1:
                            pair = PAIRS[branch]
                            dve.wait_ge(chunk_used, Chunk(n, 2 * O_STEPS, C_MERGE + s).number + 1)
                            dve.wait_ge(gate_ready, n * 2 + branch + 1)
                            dve.tensor_tensor(dst[:, :, :], acc[pair][:, :, :], dst[:, :, :], ALU.mult)\
                               .then_inc(evacuated[pair], 1)
                    if s == 2 * O_STEPS - 1:
                        for pair in PAIRS:
                            dve.wait_ge(evacuated[pair], n + U_MERGE + 1)
                        dve.tensor_tensor(merge_y[:, :, :], merge[0][:, :, :], merge[1][:, :, :], ALU.add)\
                           .then_inc(merged, 1)
                    rest_of_chunk(Chunk(n, 2 * O_STEPS, C_MERGE + s + RING))

            merge_steps(0, True)
            with dve.Fori(1, OUT_GROUPS) as n:
                merge_steps(n, False)

            def add_residual(n, last_chunk):
                pair, piece = acc[PAIRS[n % 2]], rows[:, :, n * COLS:(n + 1) * COLS]
                dve.wait_ge(chunk_used, last_chunk + 1)
                dve.tensor_tensor(piece, pair[:, :, :], piece, ALU.add).then_inc(evacuated[PAIRS[n % 2]], 1)

            for n in range(OUT_GROUPS):
                for s in range(IN_STEPS):
                    if s == 2:
                        if n == 0:
                            rest_of_block(y_high, y_low, (OUT_GROUPS - 1) * BLOCK_KT, None, B_OUT - 1)
                        else:
                            rest_of_block(x2_high, x2_low, (n - 1) * BLOCK_KT, gains[:, 1, :], B_OUT + n - 1)
                    if s == IN_STEPS - 1:
                        add_residual(n, C_OUT + (n + 1) * IN_STEPS - 1)
                    rest_of_chunk(Chunk(n, IN_STEPS, C_OUT + s + RING))

            def ff_steps(n, first):
                for s in range(2 * IN_STEPS):
                    if s == 0 and first:
                        root(1)
                    if s == 2:
                        if first:
                            rest_of_block(x2_high, x2_low, (OUT_GROUPS - 1) * BLOCK_KT, gains[:, 1, :], B_FF - 1)
                        else:
                            rest_of_block(h_high, h_low, (n - 1) * BLOCK_KT, None, n + B_FF - 1)
                    if s == 2 * IN_STEPS - 1:
                        dve.wait_ge(chunk_used, Chunk(n, 2 * IN_STEPS, C_FF + s).number + 1)
                        dve.wait_ge(evacuated[PAIRS[0]], n + U_FF + 1)
                        for t in range(TT):
                            last = dve.scalar_tensor_tensor(out=hidden_rows[:, t, :], in0=acc[PAIRS[1]][:, t, :],
                                                            scalar=rstd[:, 1, t:t + 1], in1=silu[:, t, :],
                                                            op0=ALU.mult, op1=ALU.mult)
                        last.then_inc(evacuated[PAIRS[1]], 1)
                    rest_of_chunk(Chunk(n, 2 * IN_STEPS, C_FF + s + RING))

            ff_steps(0, True)
            with dve.Fori(1, FF_GROUPS) as n:
                ff_steps(n, False)

            for n in range(OUT_GROUPS):
                for s in range(FF_STEPS):
                    if n == 0 and s == 2:
                        rest_of_block(h_high, h_low, (FF_GROUPS - 1) * BLOCK_KT, None, B_FF + FF_GROUPS - 1)
                        dve.wait_ge(fin_landed, 16)
                    if s == FF_STEPS - 1 and n < OUT_GROUPS - 1:
                        add_residual(n, C_DOWN + (n + 1) * FF_STEPS - 1)
                        dve.wait_ge(evacuated[PAIRS[n % 2]], U_DOWN + n // 2 + 1)
                        gain = final_gain[:, n * COLS:(n + 1) * COLS].unsqueeze(1).broadcast_to([P, TT, COLS])
                        dve.tensor_tensor(scaled_rows[:, :, n * COLS:(n + 1) * COLS],
                                          rows[:, :, n * COLS:(n + 1) * COLS], gain, ALU.mult)\
                           .then_inc(final_scaled, 1)
                    if C_DOWN + n * FF_STEPS + s + RING < CHUNKS:
                        rest_of_chunk(Chunk(0, RING, C_DOWN + n * FF_STEPS + s + RING))
            cols = slice(D - COLS, D)
            for t in range(TT):
                if t == 0:
                    dve.wait_ge(tile_done, 1)
                else:
                    dve.wait_ge(chunk_used, CHUNKS)
                dve.tensor_tensor(rows[:, t, cols], acc[PAIRS[(OUT_GROUPS - 1) % 2]][:, t, :], rows[:, t, cols],
                                  ALU.add).then_inc(rows_added, 1)
                dve.wait_ge(rows_added, t + 1)
                dve.tensor_tensor(scaled_rows[:, t, cols], rows[:, t, cols], final_gain[:, cols], ALU.mult)\
                   .then_inc(final_scaled, 1)
                root(2 + t, slice(t, t + 1))
                dve.wait_ge(final_scaled, OUT_GROUPS + t)
                for a, b in DVE_RESULT:
                    piece = scaled_rows[:, t, a:b]
                    dve.tensor_scalar(piece, piece, rstd[:, 2 + t, t:t + 1], None, ALU.mult).then_inc(result_dve, 1)

        @block.tensor
        def _(pe):
            def multiply(chunk, high, low, kt, pair, first, last, tiles=range(TT), done=chunk_used):
                pe.wait_ge(raw_free, split_count(chunk))
                for k in range(CHUNK_KT):
                    for t in tiles:
                        x_h = high[:, kt + k, t * P:(t + 1) * P]
                        x_l = low[:, kt + k, t * P:(t + 1) * P]
                        w_h, w_l = weight_high[:, chunk.slot, k, :], weight_low[:, chunk.slot, k, :]
                        o = acc[pair][:, t, :]
                        pe.matmul(o, x_h, w_h, start=first and k == 0, stop=False)
                        pe.matmul(o, x_h, w_l, start=False, stop=False)
                        mm = pe.matmul(o, x_l, w_h, start=False, stop=last and k == CHUNK_KT - 1)
                if done is not None:
                    mm.then_inc(done, 1)

            def turn_block(src, pair, what=block_turned):
                for j in range(BLOCK_KT):
                    for t in range(TT):
                        last = pe.transpose(pair[:, j // 2, (j % 2) * TOKENS + t * P:(j % 2) * TOKENS + (t + 1) * P],
                                            src[:, t, j * P:(j + 1) * P], identity[:, :])
                last.then_inc(what, 1)

            pe.wait_ge(consts, 1)
            for n in range(WARM_UP):
                pe.transpose(turn[:, 0, 0:P], identity[:, :], identity[:, :])
            pe.wait_ge(consts, 6)
            pe.wait_ge(gain_landed, 32)
            for n in range(2):
                last = pe.transpose(ps_gain[:, n, :], gain_rows[:, n, :], identity[0:KT, 0:KT])
            last.then_inc(gains_turned, 1)
            def forget_block(b):
                pe.wait_ge(x_split, (b + 1) * BLOCK_KT)
                for kt in range(b * BLOCK_KT, (b + 1) * BLOCK_KT):
                    for n, (w, xt) in enumerate(((w_forget_high, x_high), (w_forget_low, x_high),
                                                 (w_forget_high, x_low))):
                        last = pe.matmul(ps_forget_turned, w[:, kt, :], xt[:, kt, :], start=kt == 0 and n == 0,
                                         stop=kt == KT - 1 and n == 2)
                if b == KT // BLOCK_KT - 1:
                    last.then_inc(forget_multiplied, 1)

            for b in range(KT // BLOCK_KT):
                pe.wait_ge(x_landed[b], 16)
                if b == 2:
                    pe.wait_ge(evacuated[1], 1)
                if b == 3:
                    pe.wait_ge(x_split, BLOCK_KT)
                turn_block(rows[:, :, b * COLS:(b + 1) * COLS], turned_x[b], x_turned)
            pe.wait_ge(wf_split, 1)
            for b in range(KT // BLOCK_KT - 1):
                forget_block(b)
            forget_block(KT // BLOCK_KT - 1)
            pe.wait_ge(forget_taken, 1)
            for t in range(TT):
                last = pe.transpose(ps_forget[:, t, :], forget_turned[:, t * P:(t + 1) * P],
                                    identity[0:HEADS, 0:HEADS])
            last.then_inc(forget_logits, 1)

            def sum_decay(it):
                pe.wait_ge(decay_split, it + 1)
                pe.wait_ge(evacuated[2], it + 1)
                n = GROUP_HEADS
                terms = [(0, 0, up_to[:, 0:P]), (n, 0, up_to[:, 2 * P:3 * P]), (n, 1, up_to[:, 0:P])]
                for k, (o, t, ones) in enumerate(terms):
                    for part in (decay_high, decay_low):
                        last = pe.matmul(ps_probs[:, o:o + n], ones, part[:, t, :],
                                         start=k < 2 and part is decay_high, stop=k != 1 and part is decay_low)
                last.then_inc(decay_summed, 1)

            def turn_qk(it, h, head):
                pair_q, use_q = pair_use(Q_G, it)
                pair_k, use_k = pair_use(K_G, it)
                pe.wait_ge(evacuated[pair_k], use_k + 1)
                pe.wait_ge(evacuated[pair_q], use_q + 1)
                for n, src in enumerate((q_rows, k_rows)):
                    for t in range(TT):
                        last = pe.transpose(ps_qk[:, n * TOKENS + t * P:n * TOKENS + (t + 1) * P],
                                            src[:, t, h * HEAD:(h + 1) * HEAD], identity[:, :])
                last.then_inc(qk_in_psum, 1)

            def scores(branch, h, head):
                if branch == 0:
                    for part in (decay_high, decay_low):
                        minus = [part[:, u, h:h + 1].broadcast_to([P, P]) for u in range(TT)]
                        pe.matmul(ps_scores[:, 0:3 * P], minus[0], up_to[:, :], start=part is decay_high, stop=False)
                        pe.matmul(ps_scores[:, 2 * P:3 * P], minus[1], up_to[:, 0:P], start=False, stop=False)
                pe.wait_ge(qk_split, head + 1)
                for t, (a, b) in enumerate(((0, P), (P, 3 * P))):
                    mine, keys = slice(t * P, (t + 1) * P), slice(0, b - a)
                    for n, (q, k) in enumerate(((qk_high, qk_high), (qk_high, qk_low), (qk_low, qk_high))):
                        last = pe.matmul(ps_scores[:, a:b], q[:, 0, mine], k[:, 1, keys],
                                         start=branch == 1 and n == 0, stop=n == 2 and (branch == 1 or t == TT - 1))
                last.then_inc(scores_in_psum, 1)

            def turn_probs(head):
                pe.wait_ge(probs_ready, head + 1)
                for n in range(3):
                    last = pe.transpose(ps_probs[:, n * P:(n + 1) * P], probs[:, n * P:(n + 1) * P], identity[:, :])
                last.then_inc(p_in_psum, 1)

            def values(it, h, head):
                pair_v, use_v = pair_use(V_G, it)
                pe.wait_ge(evacuated[pair_v], use_v + 1)
                pe.wait_ge(p_split, head + 1)
                cols = slice(h * HEAD, (h + 1) * HEAD)
                for n, (v, p) in enumerate(((v_high, p_high), (v_high, p_low), (v_low, p_high))):
                    pe.matmul(ps_o[:, 0:TOKENS], v[:, 0, cols], p[:, 0:TOKENS], start=n == 0, stop=False)
                    last = pe.matmul(ps_o[:, P:TOKENS], v[:, 1, cols], p[:, TOKENS:3 * P], start=False, stop=n == 2)
                last.then_inc(o_in_psum, 1)

            for branch in range(2):
                with pe.Fori(0, HALVES) as half:
                    it = half + HALVES * branch
                    for s in range(HALF_STEPS):
                        g, c = divmod(s, IN_STEPS)
                        if branch == 0 and s == IN_STEPS + 1:
                            sum_decay(it)
                        for h in range(GROUP_HEADS):
                            head = it * GROUP_HEADS + h
                            at_step = s - HEAD_STEPS * h
                            if at_step == VALUES:
                                values(it, h, head)
                            if at_step == VALUES + 1:
                                pe.wait_ge(o_split, head + 1)
                            if at_step == TURN_QK[h]:
                                turn_qk(it, h, head)
                            if at_step == SCORES:
                                scores(branch, h, head)
                        for h in range(GROUP_HEADS):
                            if s - HEAD_STEPS * h == TURN_P:
                                turn_probs(it * GROUP_HEADS + h)
                        pair, use = pair_use(g, it)
                        if c == 0 and g != K_G:
                            pe.wait_ge(evacuated[pair], use)
                        multiply(Chunk(half, HALF_STEPS, HALVES * branch * HALF_STEPS + s), x_high, x_low,
                                 c * CHUNK_KT, pair, c == 0, c == IN_STEPS - 1)

            def merge_steps(n, first):
                for s in range(2 * O_STEPS):
                    branch, c = divmod(s, O_STEPS)
                    if s == 2 and not first:
                        pe.wait_ge(merged, n)
                        turn_block(merge_y, turn)
                    if s == 2 * O_STEPS - 1 and not first:
                        pe.wait_ge(block_split, n)
                    if c == 0:
                        pe.wait_ge(o_split, (branch + 1) * HEADS)
                        pe.wait_ge(evacuated[PAIRS[branch]], n + U_MERGE)
                    multiply(Chunk(n, 2 * O_STEPS, C_MERGE + s), o_high, o_low,
                             branch * HEADS + c * CHUNK_KT, PAIRS[branch], c == 0, c == O_STEPS - 1)

            merge_steps(0, True)
            with pe.Fori(1, OUT_GROUPS) as n:
                merge_steps(n, False)

            for n in range(OUT_GROUPS):
                pair, use = PAIRS[n % 2], U_OUT + n // 2
                for s in range(IN_STEPS):
                    if s == 2:
                        pe.wait_ge(block_split, B_OUT + n - 1)
                        if n == 0:
                            pe.wait_ge(merged, OUT_GROUPS)
                            turn_block(merge_y, turn)
                        else:
                            pe.wait_ge(evacuated[1 - pair], U_OUT + (n - 1) // 2 + 1)
                            turn_block(rows[:, :, (n - 1) * COLS:n * COLS], turn)
                    if s == 0:
                        pe.wait_ge(block_split, B_OUT - 1)
                        pe.wait_ge(evacuated[pair], use)
                    if s == IN_STEPS - BLOCK_KT // CHUNK_KT:
                        pe.wait_ge(block_split, B_OUT)
                    multiply(Chunk(n, IN_STEPS, C_OUT + s), y_high, y_low, s * CHUNK_KT, pair,
                             s == 0, s == IN_STEPS - 1)

            def ff_steps(n, first):
                for s in range(2 * IN_STEPS):
                    which, c = divmod(s, IN_STEPS)
                    pair = PAIRS[which]
                    if s == 2:
                        pe.wait_ge(block_split, n + B_FF - 1)
                        if first:
                            pe.wait_ge(evacuated[PAIRS[1]], U_FF)
                            turn_block(rows[:, :, D - COLS:D], turn)
                        else:
                            pe.wait_ge(evacuated[PAIRS[1]], n + U_FF)
                            turn_block(hidden_rows, turn)
                    if s == 0:
                        pe.wait_ge(block_split, B_FF - 1)
                    if c == 0:
                        pe.wait_ge(evacuated[pair], n + U_FF)
                    if s == IN_STEPS - BLOCK_KT // CHUNK_KT and first:
                        pe.wait_ge(block_split, B_FF)
                    multiply(Chunk(n, 2 * IN_STEPS, C_FF + s), x2_high, x2_low, c * CHUNK_KT, pair,
                             c == 0, c == IN_STEPS - 1)

            ff_steps(0, True)
            with pe.Fori(1, FF_GROUPS) as n:
                ff_steps(n, False)

            for n in range(OUT_GROUPS):
                pair, chunk = PAIRS[n % 2], lambda c: Chunk(0, RING, C_DOWN + n * FF_STEPS + c)
                whole = FF_STEPS - (RING if n == OUT_GROUPS - 1 else 0)
                for c in range(whole):
                    if n == 0 and c == 2:
                        pe.wait_ge(evacuated[PAIRS[1]], U_DOWN)
                        pe.wait_ge(block_split, B_FF + FF_GROUPS - 1)
                        turn_block(hidden_rows, turn)
                    if c == 0:
                        pe.wait_ge(evacuated[pair], n // 2 + U_DOWN)
                    if c == FF_STEPS - BLOCK_KT // CHUNK_KT:
                        pe.wait_ge(block_split, B_FF + FF_GROUPS)
                    multiply(chunk(c), h_high, h_low, c * CHUNK_KT, pair, c == 0, c == FF_STEPS - 1)
            for t in range(TT):
                for c in range(whole, FF_STEPS):
                    multiply(chunk(c), h_high, h_low, c * CHUNK_KT, pair, False, c == FF_STEPS - 1, (t,),
                             chunk_used if t == TT - 1 else tile_done if c == FF_STEPS - 1 else None)


_INS = ["x", "norm_mix", "w_in", "b_forget", "w_o_fox", "w_o_moba", "w_out", "norm_ffn", "w_gate_up", "w_down",
        "norm_final"]


def kernel(**inputs):
    import numpy as np
    import concourse.bacc as bacc
    from concourse.bass_utils import run_bass_kernel_spmd

    half = HEAD // 2
    inv_freq = np.float32(10000.0) ** (-np.arange(half, dtype=np.float32) / np.float32(half))
    angle = np.arange(TOKENS, dtype=np.float32)[:, None] * inv_freq[None, :].astype(np.float32)
    arrays = {name: np.ascontiguousarray(inputs[name]) for name in _INS}
    arrays["rope_cos"] = np.cos(angle).astype(np.float32)
    arrays["rope_sin"] = np.sin(angle).astype(np.float32)
    nc = bacc.Bacc("TRN2", target_bir_lowering=False, num_devices=1)
    args = [nc.dram_tensor(f"in_{name}", a.shape, F32, kind="ExternalInput").ap() for name, a in arrays.items()]
    args.append(nc.dram_tensor("out", (1, TOKENS, D), F32, kind="ExternalOutput").ap())
    build(nc, *args)
    r = run_bass_kernel_spmd(nc, [{f"in_{name}": a for name, a in arrays.items()}], core_ids=[0])
    return r.results[0]["out"]
```
